# Optimizing a Trainium2 kernel written in Bass

```python
import math
import jax, jax.numpy as jnp
from jax import lax
import numpy as np

D_MODEL = 4096
BATCH = 1
SEQ = 256
DEPTH = 1

MEM_LEN = 256
MIX_WIDTH = D_MODEL
DIFF_WIDTH = MIX_WIDTH // 2
FOURIER_WIDTH = MIX_WIDTH // 4
MEM_WIDTH = MIX_WIDTH - DIFF_WIDTH - FOURIER_WIDTH
DIFF_HEAD_DIM = 128
DIFF_HEADS = DIFF_WIDTH // (2 * DIFF_HEAD_DIM)
DIFF_V_DIM = 2 * DIFF_HEAD_DIM
FOURIER_GROUPS = 4
FOURIER_GROUP_DIM = FOURIER_WIDTH // FOURIER_GROUPS
MEM_HEADS = 4
MEM_HEAD_DIM = MEM_WIDTH // MEM_HEADS
Q_BLOCK = 128
RMS_EPS = 1e-6
LAMBDA_STD = 0.1
SPLIT_WIDTHS = (DIFF_WIDTH, DIFF_WIDTH, DIFF_WIDTH, DIFF_WIDTH,
                FOURIER_WIDTH, FOURIER_WIDTH,
                MEM_WIDTH, MEM_WIDTH)
IN_COLS = 4 * DIFF_WIDTH + 2 * FOURIER_WIDTH + 2 * MEM_WIDTH

kernel_name = 'hybrid_diffattn_fnet_memxattn_encoder'

def rms_norm(x, g):
    xf = x.astype(jnp.float32)
    y = xf * lax.rsqrt(jnp.mean(xf * xf, axis=-1, keepdims=True) + RMS_EPS)
    return (y * g.astype(jnp.float32)).astype(x.dtype)

def alibi_slopes(n_heads):
    return jnp.asarray([2.0 ** (-8.0 * (h + 1) / n_heads) for h in range(n_heads)], dtype=jnp.float32)

def diff_attention(q, k, v, lam, slopes):
    B, S = q.shape[0], q.shape[1]
    nb = S // Q_BLOCK
    scale = DIFF_HEAD_DIM ** -0.5
    q_blocks = jnp.moveaxis(q.reshape(B, nb, Q_BLOCK, DIFF_HEADS, 2, DIFF_HEAD_DIM), 1, 0)
    starts = jnp.arange(nb, dtype=jnp.int32) * Q_BLOCK
    k_pos = jnp.arange(S, dtype=jnp.int32)

    def one_block(args):
        qb, start = args
        s = jnp.einsum('bqhcd,bkhcd->bhcqk', qb, k, preferred_element_type=jnp.float32) * scale
        q_pos = start + jnp.arange(Q_BLOCK, dtype=jnp.int32)
        dist = jnp.abs(q_pos[:, None] - k_pos[None, :]).astype(jnp.float32)
        s = s - slopes[None, :, None, None, None] * dist[None, None, None]
        p = jax.nn.softmax(s, axis=-1)
        w = p[:, :, 0] - lam * p[:, :, 1]
        return jnp.einsum('bhqk,bkhe->bqhe', w.astype(v.dtype), v)

    out = lax.map(one_block, (q_blocks, starts))
    return jnp.moveaxis(out, 0, 1).reshape(B, S, DIFF_HEADS, DIFF_V_DIM)

def hybrid_layer(x, mem, g_in, w_in, g_mem, w_mem_k, w_mem_v, lam_q1, lam_k1, lam_q2, lam_k2,
                 g_subln, w_fourier, w_out, layer_idx, slopes):
    B, S, _ = x.shape
    h = rms_norm(x, g_in)
    proj = h @ w_in
    offsets = [int(o) for o in np.cumsum(SPLIT_WIDTHS)[:-1]]
    q_d, k_d, v_d, z_d, u_f, z_f, q_m, z_m = jnp.split(proj, offsets, axis=-1)

    lam_init = 0.8 - 0.6 * math.exp(-0.3 * layer_idx)
    lam = (jnp.exp(jnp.sum(lam_q1.astype(jnp.float32) * lam_k1.astype(jnp.float32)))
           - jnp.exp(jnp.sum(lam_q2.astype(jnp.float32) * lam_k2.astype(jnp.float32))) + lam_init)
    q = q_d.reshape(B, S, DIFF_HEADS, 2, DIFF_HEAD_DIM)
    k = k_d.reshape(B, S, DIFF_HEADS, 2, DIFF_HEAD_DIM)
    v = v_d.reshape(B, S, DIFF_HEADS, DIFF_V_DIM)
    o_d = diff_attention(q, k, v, lam, slopes)
    o_d = rms_norm(o_d, g_subln) * (1.0 - lam_init)
    y_d = o_d.reshape(B, S, DIFF_WIDTH) * jax.nn.silu(z_d)

    u = u_f.reshape(B, S, FOURIER_GROUPS, FOURIER_GROUP_DIM).astype(jnp.float32)
    f = jnp.fft.fft2(u, axes=(1, 3), norm='ortho').real.astype(x.dtype).reshape(B, S, FOURIER_WIDTH)
    y_f = (f @ w_fourier) * jax.nn.silu(z_f)

    m = rms_norm(mem, g_mem)
    km = (m @ w_mem_k).reshape(B, MEM_LEN, MEM_HEADS, MEM_HEAD_DIM)
    vm = (m @ w_mem_v).reshape(B, MEM_LEN, MEM_HEADS, MEM_HEAD_DIM)
    qm = q_m.reshape(B, S, MEM_HEADS, MEM_HEAD_DIM)
    sm = jnp.einsum('bshd,bmhd->bhsm', qm, km, preferred_element_type=jnp.float32) * (MEM_HEAD_DIM ** -0.5)
    pm = jax.nn.softmax(sm, axis=-1)
    o_m = jnp.einsum('bhsm,bmhd->bshd', pm.astype(vm.dtype), vm).reshape(B, S, MEM_WIDTH)
    y_m = o_m * jax.nn.silu(z_m)

    y = jnp.concatenate([y_d, y_f, y_m], axis=-1)
    return x + y @ w_out

def setup_inputs(seed: int = 0) -> dict:
    key = jax.random.key(seed)
    ks = jax.random.split(key, 16)
    f32 = jnp.float32
    x = jax.random.normal(ks[0], (BATCH, SEQ, D_MODEL), f32)
    mem = jax.random.normal(ks[1], (BATCH, MEM_LEN, D_MODEL), f32)
    g_in = 1.0 + 0.02 * jax.random.normal(ks[2], (DEPTH, D_MODEL), f32)
    w_in = jax.random.normal(ks[3], (DEPTH, D_MODEL, IN_COLS), f32) * D_MODEL ** -0.5
    g_mem = 1.0 + 0.02 * jax.random.normal(ks[4], (DEPTH, D_MODEL), f32)
    w_mem_k = jax.random.normal(ks[5], (DEPTH, D_MODEL, MEM_WIDTH), f32) * D_MODEL ** -0.5
    w_mem_v = jax.random.normal(ks[6], (DEPTH, D_MODEL, MEM_WIDTH), f32) * D_MODEL ** -0.5
    lam_q1 = LAMBDA_STD * jax.random.normal(ks[7], (DEPTH, DIFF_HEAD_DIM), f32)
    lam_k1 = LAMBDA_STD * jax.random.normal(ks[8], (DEPTH, DIFF_HEAD_DIM), f32)
    lam_q2 = LAMBDA_STD * jax.random.normal(ks[9], (DEPTH, DIFF_HEAD_DIM), f32)
    lam_k2 = LAMBDA_STD * jax.random.normal(ks[10], (DEPTH, DIFF_HEAD_DIM), f32)
    g_subln = 1.0 + 0.02 * jax.random.normal(ks[11], (DEPTH, DIFF_V_DIM), f32)
    w_fourier = jax.random.normal(ks[12], (DEPTH, FOURIER_WIDTH, FOURIER_WIDTH), f32) * FOURIER_WIDTH ** -0.5
    w_out = jax.random.normal(ks[13], (DEPTH, MIX_WIDTH, D_MODEL), f32) * MIX_WIDTH ** -0.5
    g_final = 1.0 + 0.02 * jax.random.normal(ks[14], (D_MODEL,), f32)
    return {'x': x, 'mem': mem, 'g_in': g_in, 'w_in': w_in, 'g_mem': g_mem, 'w_mem_k': w_mem_k,
            'w_mem_v': w_mem_v, 'lam_q1': lam_q1, 'lam_k1': lam_k1, 'lam_q2': lam_q2, 'lam_k2': lam_k2,
            'g_subln': g_subln, 'w_fourier': w_fourier, 'w_out': w_out, 'g_final': g_final}

def reference(x, mem, g_in, w_in, g_mem, w_mem_k, w_mem_v, lam_q1, lam_k1, lam_q2, lam_k2,
              g_subln, w_fourier, w_out, g_final):
    slopes = alibi_slopes(DIFF_HEADS)
    h = x
    for l in range(DEPTH):
        h = hybrid_layer(h, mem, g_in[l], w_in[l], g_mem[l], w_mem_k[l], w_mem_v[l],
                         lam_q1[l], lam_k1[l], lam_q2[l], lam_k2[l], g_subln[l],
                         w_fourier[l], w_out[l], l, slopes)
    return rms_norm(h, g_final)


_drawn_inputs = setup_inputs


def setup_inputs(seed=0):
    import zlib

    import numpy as np

    out = dict(_drawn_inputs(seed))
    spreads = {}
    factors = {'g_in': 4.2,
     'g_mem': 8.0,
     'lam_k1': 45.6,
     'lam_q2': 5.559,
     'lam_k2': 3.766,
     'g_subln': 30.589,
     'g_final': 7.747,
     'lam_q1': 3.979}
    for name, (base, spread) in spreads.items():
        noise = np.random.default_rng([zlib.crc32(name.encode()), seed]).standard_normal(out[name].shape)
        drawn = base * np.exp(spread * noise) if base else spread * noise
        out[name] = __import__('jax').numpy.asarray(drawn.astype(out[name].dtype))
    for name, factor in factors.items():
        out[name] = (out[name] * factor).astype(out[name].dtype)
    return out
```

```python
import numpy as np
from contextlib import ExitStack

import concourse.bass as bass
from concourse import mybir

P = 128
D = 4096
T = 2
SEQ = T * P
CH = 512
KT = D // P
SLAB_KT = 2
SLABS = KT // SLAB_KT
RING = 4
F_WIDTH = D // 4
F_SLABS = F_WIDTH // P // SLAB_KT
HD = 256
N_PIECES = 16
LAG = 5
EPS = 1e-6
LAM_INIT = 0.8 - 0.6
DIFF_COLS, F_COLS, M_COLS = D // 2, D // 4, D // 4
COL_Q, COL_K, COL_V, COL_Z = 0, DIFF_COLS, 2 * DIFF_COLS, 3 * DIFF_COLS
COL_U = 4 * DIFF_COLS
COL_ZF = COL_U + F_COLS
COL_QM = COL_ZF + F_COLS
COL_ZM = COL_QM + M_COLS
DIFF_SCALE = 128.0 ** -0.5
MEM_SCALE = 256.0 ** -0.5
Y_ORDER = [6, 7, 0, 1, 2, 3, 4, 5]
J_QM, J_ZM, J_DIFF, J_U, J_ZF, J_WF = 4, 6, 8, 24, 26, 28
N_WF = J_WF * SLABS
N_OUT = N_WF + 2 * F_SLABS
OUT_JOBS = D // CH


def hybrid_kernel(nc, x, mem, g_in, w_in, g_mem, w_mem_k, w_mem_v, lam_q1, lam_k1, lam_q2, lam_k2,
                  g_subln, w_fourier, w_out, g_final, dist_c, slope_c, dft_c, out):
    f32, f32r = mybir.dt.float32, mybir.dt.float32r
    ALU, ACT, AX = mybir.AluOpType, mybir.ActivationFunctionType, mybir.AxisListType
    ds = bass.ds
    ctx = ExitStack()
    with ctx:
        KB = 1024

        def at(name, shape, dt, offset):
            return nc.alloc_sbuf_tensor_at(name, shape, dt, offset=offset)

        BASE = -(-nc.sbuf_base // 32) * 32
        A, B = BASE, BASE + 64 * KB
        RAW, HI, LO = BASE + 128 * KB, BASE + 144 * KB, BASE + 160 * KB
        W = BASE + 176 * KB
        SMALL = W + 28 * KB
        OV_HI, OV_LO = B + 24 * KB, B + 56 * KB

        xT_hi = at("xT_hi", [P, KT, SEQ], f32r, A)
        xT_lo = at("xT_lo", [P, KT, SEQ], f32r, A + 32 * KB)
        mT_hi = at("mT_hi", [P, KT, SEQ], f32r, B)
        mT_lo = at("mT_lo", [P, KT, SEQ], f32r, B + 32 * KB)
        yT_hi = at("yT_hi", [P, KT, SEQ], f32r, B)
        yT_lo = at("yT_lo", [P, KT, SEQ], f32r, B + 32 * KB)
        raw = at("raw", [P, RING, SLAB_KT, CH], f32, RAW)
        w_hi = at("w_hi", [P, RING, SLAB_KT, CH], f32r, HI)
        w_lo = at("w_lo", [P, RING, SLAB_KT, CH], f32r, LO)

        nat = at("nat", [P, T, CH], f32, W)
        qT = at("qT", [P, 4, SEQ], f32, W + 4 * KB)
        gate = at("gate", [P, T, CH], f32, W + 8 * KB)
        kmT = at("kmT", [P, 8, SEQ], f32, W + 12 * KB)
        vm = at("vm", [P, T, F_WIDTH], f32, W + 20 * KB)
        kT = at("kT", [P, 4, SEQ], f32, W + 12 * KB)
        v = at("v", [P, T, CH], f32, W + 16 * KB)
        lam_vecs = at("lam_vecs", [P, 4, P], f32, W)
        g_rows = at("g_rows", [KT, 2, P], f32, W + 2 * KB)
        stage = at("stage", [P, 4, T, SLAB_KT * P], f32, W + 4 * KB)
        fT_hi = at("fT_hi", [P, 8, SEQ], f32r, W + 12 * KB)
        fT_lo = at("fT_lo", [P, 8, SEQ], f32r, W + 20 * KB)
        gate1 = at("gate1", [P, T, CH], f32, W)
        dft = at("dft", [P, T, 2 * SEQ], f32, W + 4 * KB)
        probs = at("probs", [P, 2, 2, T, SEQ], f32, OV_HI)
        pT = at("pT", [P, 2, T, SEQ], f32, OV_LO)
        dist = at("dist", [P, T, SEQ], f32, OV_LO + 4 * KB)
        gsub = at("gsub", [P, HD], f32, OV_LO + 6 * KB)
        u = at("u", [P, 2, T, CH], f32, OV_HI)
        aT = at("aT", [P, 4, 2, SEQ], f32, OV_LO)
        acc_out = at("acc_out", [P, T, D], f32, A)
        g_fin = at("g_fin", [P, D], f32, A + 32 * KB)
        junk_out = at("junk_out", [P, T, CH], f32, A + 48 * KB)

        small_at = [SMALL]

        def small(name, shape):
            h = at(name, shape, f32, small_at[0])
            small_at[0] += -(-4 * int(np.prod(shape[1:])) // 32) * 32
            return h

        ident = small("ident", [P, P])
        junk = small("junk", [P, T, SEQ])
        gT = small("gT", [P, 2, KT])
        ssq = small("ssq", [P, 2, T, N_PIECES])
        ms = small("ms", [P, 2, T])
        rstd = small("rstd", [P, 2, T])
        rstd_neg = small("rstd_neg", [P, T])
        rstd_q = small("rstd_q", [P, T])
        rstd_qm = small("rstd_qm", [P, T])
        half = small("half", [P, 8])
        eps = small("eps", [P, 2, T])
        slopes = small("slopes", [P, 8])
        lam_prod = small("lam_prod", [P, 2, 1])
        lam_neg = small("lam_neg", [P, 1])
        negmax = small("negmax", [P, 2, 2, T])
        rowsum = small("rowsum", [P, 2, 2, T])
        rinv = small("rinv", [P, 2, 2, T])
        rinv_mem = small("rinv_mem", [P, 2, 2, T])
        ssq_o = small("ssq_o", [P, 2, T])
        rstd_o = small("rstd_o", [P, 2, T])
        ssq_f = small("ssq_f", [P, T, OUT_JOBS])
        ms_f = small("ms_f", [P, T])
        rstd_f = small("rstd_f", [P, T])
        assert small_at[0] <= nc.sbuf_top

        acc = [ctx.enter_context(nc.psum_tensor(f"acc{i}", [P, T, CH], f32)) for i in range(2)]
        X = [ctx.enter_context(nc.psum_tensor(f"aux{i}", [P, CH], f32)) for i in range(4)]

        def sem(name):
            return ctx.enter_context(nc.semaphore(name))

        raw_landed = [sem(f"raw_landed{i}") for i in range(RING)]
        hi_ready = sem("hi_ready")
        lo_ready = sem("lo_ready")
        slab_used = sem("slab_used")
        piece_landed = [sem(f"piece_landed{i}") for i in range(4)]
        piece_transposed = sem("piece_transposed")
        piece_squared = sem("piece_squared")
        piece_hi = sem("piece_hi")
        piece_lo = sem("piece_lo")
        evac_act = sem("evac_act")
        evac_dve = sem("evac_dve")
        nat_transposed = sem("nat_transposed")
        natT_act = sem("natT_act")
        natT_dve = sem("natT_dve")
        scores_done = sem("scores_done")
        max_ready = sem("max_ready")
        exp_ready = sem("exp_ready")
        probs_ready = sem("probs_ready")
        probs_transposed = sem("probs_transposed")
        pT_act = sem("pT_act")
        pT_dve = sem("pT_dve")
        pv_done = sem("pv_done")
        ssq_o_ready = sem("ssq_o_ready")
        rstd_o_ready = sem("rstd_o_ready")
        y_ready = sem("y_ready")
        y_transposed = sem("y_transposed")
        yT_hi_ready = sem("yT_hi_ready")
        yT_lo_ready = sem("yT_lo_ready")
        dft_pos_done = sem("dft_pos_done")
        aT_act = sem("aT_act")
        aT_dve = sem("aT_dve")
        dft_chan_done = sem("dft_chan_done")
        fT_hi_ready = sem("fT_hi_ready")
        fT_lo_ready = sem("fT_lo_ready")
        small_landed = sem("small_landed")
        const_landed = sem("const_landed")
        dft_landed = sem("dft_landed")
        resid_landed = sem("resid_landed")
        ident_ready = sem("ident_ready")
        g_transposed = sem("g_transposed")
        gT_ready = sem("gT_ready")
        ssq_ready = sem("ssq_ready")
        ms_ready = sem("ms_ready")
        rstd_ready = sem("rstd_ready")
        lam_sums = sem("lam_sums")
        lam_exp = sem("lam_exp")
        squared_out = sem("squared_out")
        summed_out = sem("summed_out")
        scaled_out = sem("scaled_out")
        ssq_f_ready = sem("ssq_f_ready")
        rstd_f_ready = sem("rstd_f_ready")
        stored = sem("stored")
        act_done_out = sem("act_done_out")
        dve_done_out = sem("dve_done_out")
        pool_step = sem("pool_step")
        lam_step = sem("lam_step")
        gate_step = sem("gate_step")
        max_step = sem("max_step")
        comb_step = sem("comb_step")
        rinv_mem_ready = sem("rinv_mem_ready")
        gsub_step = sem("gsub_step")
        gsub_pool = sem("gsub_pool")
        gfin_landed = sem("gfin_landed")

        def diff_job(g, part):
            return g * 4 + (J_DIFF + part)

        def slab0(job):
            return job * SLABS

        block = ctx.enter_context(nc.Block())

        @block.sync
        def _(sp):
            def load_slab(w, row0, col, s, n0, q0):
                if not (isinstance(n0, int) and n0 + s < RING):
                    sp.wait_ge(lo_ready, n0 + (s - RING + 1))
                src = w[row0:row0 + SLAB_KT * P, :].rearrange("(k p) n -> p k n", p=P)
                sp.dma_start(raw[:, s % RING], src[:, :, ds(col, CH)]).then_inc(raw_landed[s % RING], 16)

            def load_job(w, col, job):
                for s in range(SLABS):
                    load_slab(w, s * SLAB_KT * P, col, s, slab0(job), 4 * job)

            def load_piece(i):
                src = mem if i < N_PIECES else x
                c = (i % N_PIECES) * SLAB_KT * P
                if i >= 4:
                    sp.wait_ge(piece_transposed, i - 3)
                    sp.wait_ge(piece_squared, i - 3)
                sp.dma_start(stage[:, i % 4],
                             src[:, c:c + SLAB_KT * P].rearrange("(t p) n -> p t n", p=P)
                             ).then_inc(piece_landed[i % 4], 16)

            for i in range(4):
                load_piece(i)
            for j in range(4):
                w, col = (w_mem_k, w_mem_v)[j % 2], (j // 2) * CH
                for s in range(SLABS):
                    load_slab(w, s * SLAB_KT * P, col, s, slab0(j), 4 * j)
                    n = slab0(j) + s
                    if n < SLABS:
                        load_piece(n + 4)
                    elif n >= SLABS + LAG and (n - LAG) % 2 == 0 and (n - LAG) // 2 + 12 < 2 * N_PIECES:
                        load_piece((n - LAG) // 2 + 12)
            for j, col in ((4, COL_QM), (5, COL_QM + CH), (6, COL_ZM), (7, COL_ZM + CH)):
                load_job(w_in, col, j)
            with sp.Fori(0, 4) as g:
                for part, col in enumerate((COL_Q, COL_K, COL_V, COL_Z)):
                    load_job(w_in, g * CH + col, diff_job(g, part))
            sp.wait_ge(scores_done, 6)
            sp.dma_start(dft[:], dft_c.rearrange("(t p) n -> p t n", p=P)).then_inc(dft_landed, 16)
            for j, col in ((24, COL_U), (25, COL_U + CH), (26, COL_ZF), (27, COL_ZF + CH)):
                load_job(w_in, col, j)
            for c in range(2):
                for s in range(F_SLABS):
                    n0 = N_WF + c * F_SLABS
                    load_slab(w_fourier, s * SLAB_KT * P, c * CH, s, n0, n0 // RING)
            with sp.Fori(0, OUT_JOBS) as n:
                for s in range(SLABS):
                    row = (Y_ORDER[s // 2] * 4 + (s % 2) * SLAB_KT) * P
                    col = n * CH if row else n * SLABS * (CH // SLABS)
                    load_slab(w_out, row, col, s, n * SLABS + N_OUT, 0)
            for t in range(T):
                sp.wait_ge(dve_done_out, t + 1)
                sp.dma_start(out[t * P:(t + 1) * P, 0:D // 2], acc_out[:, t, 0:D // 2]).then_inc(stored, 16)
            sp.wait_ge(stored, 16 * 4)

        @block.tensor
        def _(pe):
            def slab(s, n0, src_hi, src_lo, banks, last):
                pe.wait_ge(lo_ready, n0 + (s + 1))
                r = s % RING
                for k in range(SLAB_KT):
                    kt = s * SLAB_KT + k
                    for t in range(T):
                        o = banks[:, t, :]
                        a_hi = src_hi[:, kt, t * P:(t + 1) * P]
                        a_lo = src_lo[:, kt, t * P:(t + 1) * P]
                        end = last and k == SLAB_KT - 1
                        nc.tensor.matmul(o, a_hi, w_hi[:, r, k, :], start=(kt == 0), stop=False)
                        nc.tensor.matmul(o, a_hi, w_lo[:, r, k, :], start=False, stop=False)
                        ins = nc.tensor.matmul(o, a_lo, w_hi[:, r, k, :], start=False, stop=end)
                ins.then_inc(slab_used, 1)

            def bank_free(job):
                pe.wait_ge(evac_act, job - 1)
                pe.wait_ge(evac_dve, job - 1)

            def transposes(banks, src, blocks, block0=0):
                for b in range(blocks):
                    for t in range(T):
                        o = (b % 2) * SEQ + t * P
                        ins = nc.tensor.transpose(banks[b // 2][:, o:o + P],
                                                  src[:, t, b * P:(b + 1) * P], ident[:])
                return ins

            def transpose_nat(use, job):
                pe.wait_ge(evac_act, job + 1)
                pe.wait_ge(evac_dve, job + 1)
                transposes(X[2:4], nat, 4).then_inc(nat_transposed, 1)

            def transpose_y(slot, src, banks):
                pe.wait_ge(y_ready, slot + 1)
                transposes(banks, src, 4).then_inc(y_transposed, 1)

            def transpose_probs(use, first_map_stride):
                pe.wait_ge(probs_ready, use + 1)
                for h in range(2):
                    for kt in range(T):
                        for t in range(T):
                            ins = nc.tensor.transpose(X[h][:, kt * SEQ + t * P:kt * SEQ + (t + 1) * P],
                                                      probs[:, h, 0, t, kt * P:(kt + 1) * P], ident[:])
                ins.then_inc(probs_transposed, 1)

            def times_v(use, v_of_head):
                pe.wait_ge(pT_act, use + 1)
                pe.wait_ge(pT_dve, use + 1)
                for h in range(2):
                    for t in range(T):
                        for kt in range(T):
                            ins = nc.tensor.matmul(X[2 + h][:, t * HD:(t + 1) * HD],
                                                   pT[:, h, kt, t * P:(t + 1) * P], v_of_head(h, kt),
                                                   start=(kt == 0), stop=(kt == T - 1))
                ins.then_inc(pv_done, 1)

            pe.wait_ge(ident_ready, 2)
            pe.wait_ge(small_landed, 16 * 7)
            for i in range(2):
                ins = nc.tensor.transpose(X[0][:, i * KT:(i + 1) * KT], g_rows[:, i, :], ident[0:KT, 0:KT])
            ins.then_inc(g_transposed, 1)

            def transpose_piece(i):
                pe.wait_ge(piece_landed[i % 4], 16 * (i // 4 + 1))
                if i == 0:
                    pe.wait_ge(gT_ready, 1)
                if i >= 2:
                    pe.wait_ge(piece_lo, i - 1)
                transposes([X[i % 2]], stage[:, i % 4], 2).then_inc(piece_transposed, 1)

            transpose_piece(0)
            transpose_piece(1)
            for n in range(4 * SLABS):
                job, s = n // SLABS, n % SLABS
                if n + 2 < N_PIECES:
                    transpose_piece(n + 2)
                if n >= SLABS and n % 2 == 0 and n // 2 + 8 < 2 * N_PIECES:
                    transpose_piece(n // 2 + 8)
                if job in (1, 3) and s == 7:
                    if job == 3:
                        pe.wait_ge(natT_act, 1)
                        pe.wait_ge(natT_dve, 1)
                    transpose_nat(job // 2, job - 1)
                if n < N_PIECES:
                    pe.wait_ge(piece_lo, n + 1)
                if s == 0 and job >= 2:
                    bank_free(job)
                slab(s, slab0(job), mT_hi, mT_lo, acc[job % 2], s == SLABS - 1)

            def scores_mem(j):
                if j == 0:
                    pe.wait_ge(piece_lo, 2 * N_PIECES)
                else:
                    pe.wait_ge(pT_act, j)
                    pe.wait_ge(pT_dve, j)
                pe.wait_ge(natT_act, 3 + j)
                pe.wait_ge(natT_dve, 3 + j)
                for h in range(2):
                    for t in range(T):
                        for d in range(2):
                            ins = nc.tensor.matmul(X[h][:, t * SEQ:(t + 1) * SEQ],
                                                   qT[:, 2 * h + d, t * P:(t + 1) * P],
                                                   kmT[:, 4 * j + 2 * h + d, :], start=(d == 0), stop=(d == 1))
                ins.then_inc(scores_done, 1)

            def mem_v(j):
                return lambda h, kt: vm[:, kt, (2 * j + h) * HD:(2 * j + h + 1) * HD]

            pe.wait_ge(piece_lo, 2 * N_PIECES)
            for job in range(4, 8):
                bank_free(job)
                for s in range(SLABS):
                    if job in (5, 6) and s == 7:
                        pe.wait_ge(natT_act, job - 3)
                        pe.wait_ge(natT_dve, job - 3)
                        transpose_nat(job - 3, job - 1)
                    if job in (5, 6) and s == 13:
                        scores_mem(job - 5)
                    if job in (6, 7) and s == 6:
                        transpose_probs(job - 6, 1)
                    if job == 6 and s == 14:
                        pe.wait_ge(evac_act, 4)
                        pe.wait_ge(evac_dve, 4)
                        times_v(0, mem_v(0))
                    if job == 7 and s == 9:
                        transpose_y(0, gate, X[2:4])
                    if job == 7 and s == 15:
                        pe.wait_ge(yT_lo_ready, 1)
                        times_v(1, mem_v(1))
                    slab(s, slab0(job), xT_hi, xT_lo, acc[job % 2], s == SLABS - 1)

            def x_job(job, parity, steps):
                bank_free(job)
                for s in range(SLABS):
                    if s in steps:
                        steps[s]()
                    slab(s, slab0(job), xT_hi, xT_lo, acc[parity], s == SLABS - 1)

            def finish_step(slot):
                return {10: lambda: (pe.wait_ge(pT_act, slot + 1), pe.wait_ge(pT_dve, slot + 1),
                                     transpose_y(slot, gate, X[0:2]))}

            def scores_diff(g):
                pe.wait_ge(natT_act, g * 2 + 6)
                pe.wait_ge(natT_dve, g * 2 + 6)
                pe.wait_ge(yT_lo_ready, g + 2)
                for h in range(2):
                    for c in range(2):
                        for t in range(T):
                            b = 2 * h + c
                            ins = nc.tensor.matmul(X[b][:, t * SEQ:(t + 1) * SEQ],
                                                   qT[:, b, t * P:(t + 1) * P], kT[:, b, :],
                                                   start=True, stop=True)
                ins.then_inc(scores_done, 1)

            def rest_of_group(g):
                x_job(diff_job(g, 1), 1, {7: lambda: transpose_nat(g * 2 + 4, diff_job(g, 0))})

                def transpose_k():
                    pe.wait_ge(natT_act, g * 2 + 5)
                    pe.wait_ge(natT_dve, g * 2 + 5)
                    transpose_nat(g * 2 + 5, diff_job(g, 1))

                x_job(diff_job(g, 2), 0, {7: transpose_k, 13: lambda: scores_diff(g)})

                def pv():
                    pe.wait_ge(evac_act, diff_job(g, 2) + 1)
                    pe.wait_ge(evac_dve, diff_job(g, 2) + 1)
                    times_v(g + 2, lambda h, kt: v[:, kt, h * HD:(h + 1) * HD])

                x_job(diff_job(g, 3), 1, {7: lambda: transpose_probs(g + 2, 2), 14: pv})

            x_job(J_DIFF, 0, finish_step(1))
            with pe.Fori(0, 3) as g:
                rest_of_group(g)
                x_job(diff_job(g, 4), 0, finish_step(g + 2))
            rest_of_group(3)

            def dft_positions(c):
                pe.wait_ge(evac_act, J_U + c + 1)
                pe.wait_ge(evac_dve, J_U + c + 1)
                if c == 0:
                    pe.wait_ge(dft_landed, 16)
                    pe.wait_ge(yT_lo_ready, 6)
                else:
                    pe.wait_ge(fT_lo_ready, 1)
                    pe.wait_ge(aT_dve, 1)
                for b in range(4):
                    for k in range(T):
                        ins = nc.tensor.matmul(X[b][:], u[:, c, k, b * P:(b + 1) * P], dft[:, k, :],
                                               start=(k == 0), stop=(k == T - 1))
                ins.then_inc(dft_pos_done, 1)

            def dft_channels(c):
                pe.wait_ge(aT_act, c + 1)
                pe.wait_ge(aT_dve, c + 1)
                for co in range(4):
                    for i in range(4):
                        b, part = i // 2, i % 2
                        col = part * SEQ + (co % 2) * P
                        ins = nc.tensor.matmul(X[co // 2][:, (co % 2) * SEQ:(co % 2 + 1) * SEQ],
                                               dft[:, b, col:col + P], aT[:, (co // 2) * 2 + b, part, :],
                                               start=(i == 0), stop=(i == 3))
                ins.then_inc(dft_chan_done, 1)

            x_job(24, 0, finish_step(5))
            x_job(25, 1, {7: lambda: dft_positions(0), 14: lambda: dft_channels(0)})
            x_job(26, 0, {7: lambda: dft_positions(1), 14: lambda: dft_channels(1)})
            x_job(27, 1, {})
            pe.wait_ge(fT_lo_ready, 2)
            for c in range(2):
                bank_free(J_WF + c)
                for s in range(F_SLABS):
                    slab(s, N_WF + c * F_SLABS, fT_hi, fT_lo, acc[c], s == F_SLABS - 1)

            def out_job(n, parity, first=None):
                if first is not None:
                    pe.wait_ge(y_ready, 7 + parity)
                else:
                    pe.wait_ge(summed_out, n * 2 - 2)
                for s in range(SLABS):
                    if first and s == 3:
                        transpose_y(6, gate, X[0:2])
                    if first and s == 9:
                        transpose_y(7, gate1, X[2:4])
                    if first and s % 2 == 0:
                        pe.wait_ge(yT_lo_ready, s // 2 + 1)
                    slab(s, n * SLABS + N_OUT, yT_hi, yT_lo, acc[parity], s == SLABS - 1)

            out_job(0, 0, first=True)
            out_job(1, 1, first=False)
            with pe.Fori(1, OUT_JOBS // 2) as i:
                for parity in range(2):
                    out_job(i * 2 + parity, parity)

        @block.scalar
        def _(act):
            for i, src in enumerate((lam_q1, lam_k1, lam_q2, lam_k2)):
                act.dma_start(lam_vecs[:, i, :], bass.AP(src.tensor, src.offset, [[0, P], [1, P]])).then_inc(small_landed, 16)
            for i, src in enumerate((g_mem, g_in)):
                act.dma_start(g_rows[:, i, :], src.rearrange("a (k p) -> (a k) p", p=P)).then_inc(small_landed, 16)
            act.dma_start(slopes[:], bass.AP(slope_c.tensor, slope_c.offset, [[0, P], [1, 8]])
                          ).then_inc(small_landed, 16)

            def hi_slab(s, n0, q0):
                act.wait_ge(raw_landed[s % RING], (q0 + (s // RING + 1)) * 16)
                if not (isinstance(n0, int) and n0 + s < RING):
                    act.wait_ge(slab_used, n0 + (s - RING + 1))
                nc.scalar.activation(w_hi[:, s % RING], raw[:, s % RING], ACT.Copy).then_inc(hi_ready, 1)

            def piece(i):
                which, k0 = i // N_PIECES, (i % N_PIECES) * SLAB_KT
                dst = (mT_hi, xT_hi)[which]
                act.wait_ge(piece_landed[i % 4], 16 * (i // 4 + 1))
                act.wait_ge(piece_transposed, i + 1)
                if i == 0:
                    act.wait_ge(gT_ready, 1)
                for k in range(SLAB_KT):
                    ins = nc.scalar.activation(dst[:, k0 + k, :], X[i % 2][:, k * SEQ:(k + 1) * SEQ], ACT.Copy,
                                               scale=gT[:, which, k0 + k:k0 + k + 1])
                ins.then_inc(piece_hi, 1)
                if i:
                    act.wait_ge(piece_squared, i)
                for t in range(T):
                    ins = nc.scalar.activation(junk[:, t, :], stage[:, i % 4, t, :], ACT.Square,
                                               accum_out=ssq[:, which, t, i % N_PIECES:i % N_PIECES + 1])
                ins.then_inc(piece_squared, 1)

            def evac(job, parity, dst, scale, nat_use=None):
                act.wait_ge(slab_used, slab0(job) + SLABS)
                if nat_use is not None:
                    act.wait_ge(nat_transposed, nat_use)
                nc.scalar.activation(dst, acc[parity][:, 0, :], ACT.Copy, scale=scale).then_inc(evac_act, 1)

            def natT(use, dst):
                act.wait_ge(nat_transposed, use + 1)
                nc.scalar.activation(dst, X[2][:], ACT.Copy).then_inc(natT_act, 1)

            def pT_out(use):
                act.wait_ge(probs_transposed, use + 1)
                nc.scalar.activation(pT[:, 0], X[0][:], ACT.Copy).then_inc(pT_act, 1)

            def exp_mem(j):
                act.wait_ge(max_ready, j + 1)
                for h in range(2):
                    for t in range(T):
                        ins = nc.scalar.activation(probs[:, h, 0, t, :], X[h][:, t * SEQ:(t + 1) * SEQ], ACT.Exp,
                                                   bias=negmax[:, h, 0, t:t + 1],
                                                   accum_out=rowsum[:, h, 0, t:t + 1])
                ins.then_inc(probs_ready, 1)

            def exp_diff(g):
                act.wait_ge(max_ready, g + 3)
                for h in range(2):
                    for c in range(2):
                        for t in range(T):
                            ins = nc.scalar.activation(probs[:, h, c, t, :], probs[:, h, c, t, :], ACT.Exp,
                                                       bias=negmax[:, h, c, t:t + 1],
                                                       accum_out=rowsum[:, h, c, t:t + 1])
                ins.then_inc(exp_ready, 1)

            def gate_exp(job, parity, dst, y_before):
                act.wait_ge(slab_used, slab0(job) + SLABS)
                if not isinstance(y_before, int) or y_before:
                    act.wait_ge(y_transposed, y_before)
                for t in range(T):
                    ins = nc.scalar.activation(dst[:, t, :], acc[parity][:, t, :], ACT.Exp,
                                               scale=rstd_neg[:, t:t + 1])
                ins.then_inc(evac_act, 1)

            def yT_out(slot, banks):
                act.wait_ge(y_transposed, slot + 1)
                for i in range(2):
                    ins = nc.scalar.activation(yT_hi[:, ds(slot * 4 + 2 * i, 2), :], banks[i][:], ACT.Copy)
                ins.then_inc(yT_hi_ready, 1)

            def squares_o(g):
                act.wait_ge(pv_done, g + 3)
                for h in range(2):
                    for t in range(T):
                        ins = nc.scalar.activation(probs[:, h, 1, t, :], X[2 + h][:, t * HD:(t + 1) * HD],
                                                   ACT.Square, scale=HD ** -0.5,
                                                   accum_out=ssq_o[:, h, t:t + 1])
                ins.then_inc(ssq_o_ready, 1)

            for n in range(4 * SLABS):
                job, s = n // SLABS, n % SLABS
                if n < N_PIECES:
                    piece(n)
                i = (n - LAG) // 2 + 8
                if n >= SLABS + LAG and (n - LAG) % 2 == 0 and i < 2 * N_PIECES:
                    piece(i)
                if n == 8:
                    act.wait_ge(lam_sums, 1)
                    nc.scalar.activation(lam_prod[:], lam_prod[:], ACT.Exp).then_inc(lam_exp, 1)
                if job >= 1 and s == LAG:
                    if job == 1:
                        act.wait_ge(rstd_ready, 1)
                    if job % 2:
                        evac(job - 1, 0, nat[:, 0, :], rstd[:, 0, 0:1], job // 2)
                    else:
                        evac(job - 1, 1, vm[:, 0, (job // 2 - 1) * CH:(job // 2) * CH], rstd[:, 0, 0:1])
                if job in (1, 3) and s == 12:
                    natT(job // 2, kmT[:, 4 * (job // 2):4 * (job // 2) + 2, :])
                hi_slab(s, slab0(job), 4 * job)

            for job in range(4, 8):
                for s in range(SLABS):
                    if s == LAG:
                        if job == 4:
                            evac(3, 1, vm[:, 0, CH:], rstd[:, 0, 0:1])
                        if job == 5:
                            act.wait_ge(rstd_ready, 2)
                        if job in (5, 6):
                            evac(job - 1, (job - 1) % 2, nat[:, 0, :], rstd_qm[:, 0:1], job - 3)
                        if job == 7:
                            gate_exp(6, 0, gate, 0)
                    if job in (5, 6) and s == 12:
                        natT(job - 3, qT[:, 0:2, :])
                    if job in (6, 7) and s == 3:
                        exp_mem(job - 6)
                    if job in (6, 7) and s == 11:
                        pT_out(job - 6)
                    if job == 7 and s == 14:
                        yT_out(0, X[2:4])
                    hi_slab(s, slab0(job), 4 * job)

            def x_job(job, steps):
                for s in range(SLABS):
                    if s in steps:
                        steps[s]()
                    hi_slab(s, slab0(job), job * 4)

            def finish_steps(slot, job):
                steps = {LAG: lambda: gate_exp(job - 1, 1, gate, slot), 15: lambda: yT_out(slot, X[0:2])}
                return steps

            def rest_of_group(g):
                x_job(diff_job(g, 1), {LAG: lambda: evac(diff_job(g, 0), 0, nat[:, 0, :], rstd_q[:, 0:1], g * 2 + 4),
                                       12: lambda: natT(g * 2 + 4, qT[:, 0:2, :])})
                x_job(diff_job(g, 2), {LAG: lambda: evac(diff_job(g, 1), 1, nat[:, 0, :], rstd[:, 1, 0:1], g * 2 + 5),
                                       12: lambda: natT(g * 2 + 5, kT[:, 0:2, :])})
                x_job(diff_job(g, 3), {3: lambda: exp_diff(g),
                                       LAG + 1: lambda: evac(diff_job(g, 2), 0, v[:, 0, :], rstd[:, 1, 0:1]),
                                       12: lambda: pT_out(g + 2)})

            x_job(J_DIFF, finish_steps(1, J_DIFF))
            with act.Fori(0, 3) as g:
                rest_of_group(g)
                x_job(diff_job(g, 4), {3: lambda: squares_o(g), **finish_steps(g + 2, diff_job(g, 4))})
            rest_of_group(3)

            def aT_out(c):
                act.wait_ge(dft_pos_done, c + 1)
                for b in range(2):
                    nc.scalar.activation(aT[:, b, 0, :], X[b][:, 0:SEQ], ACT.Copy)
                    ins = nc.scalar.activation(aT[:, b, 1, :], X[b][:, SEQ:], ACT.Copy, scale=-1.0)
                ins.then_inc(aT_act, 1)

            def fT_out(c):
                act.wait_ge(dft_chan_done, c + 1)
                for i in range(2):
                    ins = nc.scalar.activation(fT_hi[:, 4 * c + 2 * i:4 * c + 2 * i + 2, :], X[i][:], ACT.Copy)
                ins.then_inc(fT_hi_ready, 1)

            x_job(24, {3: lambda: squares_o(3), **finish_steps(5, 24)})
            x_job(25, {LAG: lambda: evac(24, 0, u[:, 0, 0, :], rstd[:, 1, 0:1]), 12: lambda: aT_out(0)})
            x_job(26, {3: lambda: fT_out(0), LAG: lambda: evac(25, 1, u[:, 1, 0, :], rstd[:, 1, 0:1]),
                       12: lambda: aT_out(1)})
            x_job(27, {3: lambda: fT_out(1), LAG: lambda: gate_exp(26, 0, gate, 6)})
            for c in range(2):
                for s in range(F_SLABS):
                    if c == 1 and s == 1:
                        gate_exp(27, 1, gate1, 6)
                    hi_slab(s, N_WF + c * F_SLABS, (N_WF + c * F_SLABS) // RING)

            def squares_out(n):
                for t in range(T):
                    act.wait_ge(summed_out, n * 2 + (t + 1))
                    nc.scalar.activation(junk_out[:, t, :], acc_out[:, t, ds(n * CH, CH)], ACT.Square,
                                         accum_out=ssq_f[:, t, ds(n, 1)]).then_inc(squared_out, 1)

            def out_job(n, steps):
                for s in range(SLABS):
                    if s in steps:
                        steps[s]()
                    hi_slab(s, n * SLABS + N_OUT, n * 4 + N_OUT // RING)

            out_job(0, {8: lambda: yT_out(6, X[0:2]), 13: lambda: yT_out(7, X[2:4])})
            with act.Fori(1, OUT_JOBS) as n:
                out_job(n, {LAG + 1: lambda: squares_out(n - 1)})
            squares_out(OUT_JOBS - 1)
            act.wait_ge(rstd_f_ready, 1)
            for t in range(T):
                act.wait_ge(scaled_out, 2 * (OUT_JOBS - 1) + t + 1)
                nc.scalar.activation(acc_out[:, t, D // 2:], acc_out[:, t, D // 2:], ACT.Copy,
                                     scale=rstd_f[:, t:t + 1]).then_inc(act_done_out, 1)
                act.wait_ge(act_done_out, t + 1)
                act.dma_start(out[t * P:(t + 1) * P, D // 2:], acc_out[:, t, D // 2:]).then_inc(stored, 16)

        @block.vector
        def _(dve):
            def lo_slab(s, n0):
                dve.wait_ge(hi_ready, n0 + (s + 1))
                nc.vector.tensor_tensor(w_lo[:, s % RING], raw[:, s % RING], w_hi[:, s % RING].bitcast(f32),
                                        ALU.subtract).then_inc(lo_ready, 1)

            def piece(i):
                which, k0 = i // N_PIECES, (i % N_PIECES) * SLAB_KT
                hi, lo = ((mT_hi, mT_lo), (xT_hi, xT_lo))[which]
                dve.wait_ge(piece_hi, i + 1)
                for k in range(SLAB_KT):
                    ins = nc.vector.scalar_tensor_tensor(
                        lo[:, k0 + k, :], X[i % 2][:, k * SEQ:(k + 1) * SEQ], gT[:, which, k0 + k:k0 + k + 1],
                        hi[:, k0 + k, :].bitcast(f32), ALU.mult, ALU.subtract)
                ins.then_inc(piece_lo, 1)

            def evac(job, parity, dst, scale, nat_use=None):
                dve.wait_ge(slab_used, slab0(job) + SLABS)
                if nat_use is not None:
                    dve.wait_ge(nat_transposed, nat_use)
                nc.vector.tensor_scalar(dst, acc[parity][:, 1, :], scale, None, ALU.mult).then_inc(evac_dve, 1)

            def natT(use, dst):
                dve.wait_ge(nat_transposed, use + 1)
                nc.vector.tensor_copy(dst, X[3][:].rearrange("p (b n) -> p b n", b=2)).then_inc(natT_dve, 1)

            def pT_out(use):
                dve.wait_ge(probs_transposed, use + 1)
                nc.vector.tensor_copy(pT[:, 1], X[1][:].rearrange("p (b n) -> p b n", b=2)).then_inc(pT_dve, 1)

            def max_mem(j):
                dve.wait_ge(scores_done, j + 1)
                for h in range(2):
                    ins = nc.vector.tensor_reduce(negmax[:, h, 0, :], X[h][:].rearrange("p (t n) -> p t n", t=T),
                                                  AX.X, ALU.max, negate=True)
                ins.then_inc(max_ready, 1)

            def max_diff(g):
                dve.wait_ge(scores_done, g + 3)
                for h in range(2):
                    for c in range(2):
                        nc.vector.scalar_tensor_tensor(
                            probs[:, h, c], dist[:], slopes[:, ds(g * 2 + h, 1)],
                            X[2 * h + c][:].rearrange("p (t n) -> p t n", t=T),
                            ALU.mult, ALU.add).then_inc(max_step, 1)
                dve.wait_ge(max_step, g * 4 + 4)
                nc.vector.tensor_reduce(negmax[:], probs[:], AX.X, ALU.max, negate=True).then_inc(max_ready, 1)

            def combine(g):
                dve.wait_ge(exp_ready, g + 1)
                nc.vector.reciprocal(rinv[:], rowsum[:]).then_inc(comb_step, 1)
                dve.wait_ge(comb_step, g * 6 + 1)
                nc.vector.tensor_scalar(rinv[:, :, 1, :], rinv[:, :, 1, :], lam_neg[:, 0:1], None,
                                        ALU.mult).then_inc(comb_step, 1)
                dve.wait_ge(comb_step, g * 6 + 2)
                for h in range(2):
                    for t in range(T):
                        nc.vector.tensor_scalar(probs[:, h, 1, t, :], probs[:, h, 1, t, :],
                                                rinv[:, h, 1, t:t + 1], None, ALU.mult).then_inc(comb_step, 1)
                dve.wait_ge(comb_step, g * 6 + 6)
                for h in range(2):
                    for t in range(T):
                        ins = nc.vector.scalar_tensor_tensor(probs[:, h, 0, t, :], probs[:, h, 0, t, :],
                                                             rinv[:, h, 0, t:t + 1], probs[:, h, 1, t, :],
                                                             ALU.mult, ALU.add)
                ins.then_inc(probs_ready, 1)

            def gate_a(job, use, buf):
                dve.wait_ge(evac_act, job + 1)
                nc.vector.tensor_scalar(buf[:], buf[:], 1.0, None, ALU.add).then_inc(gate_step, 1)
                dve.wait_ge(gate_step, use * 3 + 1)
                nc.vector.reciprocal(buf[:, 0, :], buf[:, 0, :]).then_inc(gate_step, 1)

            def gate_b(use, buf):
                nc.vector.reciprocal(buf[:, 1, :], buf[:, 1, :]).then_inc(gate_step, 1)

            def gate_c(use, parity, buf, sub=None):
                dve.wait_ge(gate_step, use * 3 + 3)
                if sub is not None:
                    for t in range(T):
                        for h in range(2):
                            ins = nc.vector.tensor_tensor(buf[:, t, h * HD:(h + 1) * HD],
                                                          buf[:, t, h * HD:(h + 1) * HD], gsub[:], ALU.mult)
                            ins.then_inc(gsub_step, 1)
                    dve.wait_ge(gsub_step, sub * 4 + 4)
                for t in range(T):
                    ins = nc.vector.scalar_tensor_tensor(buf[:, t, :], acc[parity][:, t, :], rstd[:, 1, t:t + 1],
                                                         buf[:, t, :], ALU.mult, ALU.mult)
                ins.then_inc(evac_dve, 1)

            def y_attention(job, scale):
                dve.wait_ge(evac_dve, job + 1)
                for h in range(2):
                    for t in range(T):
                        g_ = gate[:, t, h * HD:(h + 1) * HD]
                        ins = nc.vector.scalar_tensor_tensor(g_, X[2 + h][:, t * HD:(t + 1) * HD],
                                                             scale(h, t), g_, ALU.mult, ALU.mult)
                ins.then_inc(y_ready, 1)

            def rinv_of_mem(j):
                dve.wait_ge(probs_ready, j + 1)
                nc.vector.reciprocal(rinv_mem[:, j], rowsum[:, :, 0, :]).then_inc(rinv_mem_ready, 1)

            def y_mem(j, job):
                dve.wait_ge(pv_done, j + 1)
                dve.wait_ge(rinv_mem_ready, j + 1)
                y_attention(job, lambda h, t: rinv_mem[:, j, h, t:t + 1])

            def y_diff(g, job):
                dve.wait_ge(rstd_o_ready, g + 1)
                y_attention(job, lambda h, t: rstd_o[:, h, t:t + 1])

            def yT_out(slot, banks):
                dve.wait_ge(yT_hi_ready, slot + 1)
                for i in range(2):
                    ins = nc.vector.tensor_tensor(yT_lo[:, ds(slot * 4 + 2 * i, 2), :],
                                                  banks[i][:].rearrange("p (b n) -> p b n", b=2),
                                                  yT_hi[:, ds(slot * 4 + 2 * i, 2), :].bitcast(f32), ALU.subtract)
                ins.then_inc(yT_lo_ready, 1)

            dve.wait_ge(g_transposed, 1)
            nc.vector.tensor_copy(gT[:], X[0][:, 0:2 * KT].rearrange("p (a k) -> p a k", a=2)).then_inc(gT_ready, 1)
            dve.wait_ge(small_landed, 16 * 7)
            for i in range(2):
                nc.vector.tensor_tensor(lam_vecs[:, 2 * i, :], lam_vecs[:, 2 * i, :], lam_vecs[:, 2 * i + 1, :],
                                        ALU.mult).then_inc(lam_step, 1)
            dve.wait_ge(lam_step, 2)
            nc.vector.tensor_reduce(lam_prod[:, :, 0], lam_vecs[:, 0:4:2, :], AX.X, ALU.add).then_inc(lam_sums, 1)

            for n in range(4 * SLABS):
                job, s = n // SLABS, n % SLABS
                if n < N_PIECES:
                    piece(n)
                i = (n - LAG) // 2 + 8
                if n >= SLABS + LAG and (n - LAG) % 2 == 0 and i < 2 * N_PIECES:
                    piece(i)
                if n == 10:
                    dve.wait_ge(lam_exp, 1)
                    nc.vector.tensor_tensor(lam_neg[:], lam_prod[:, 1, :], lam_prod[:, 0, :],
                                            ALU.subtract).then_inc(lam_step, 1)
                    dve.wait_ge(lam_step, 3)
                    nc.vector.tensor_scalar(lam_neg[:], lam_neg[:], -LAM_INIT, None, ALU.add).then_inc(lam_step, 1)
                if n in (SLABS + 1, 3 * SLABS + 8):
                    which = n // (2 * SLABS)
                    dve.wait_ge(piece_squared, (which + 1) * N_PIECES)
                    nc.vector.tensor_reduce(ms[:, which, :], ssq[:, which], AX.X, ALU.add).then_inc(ssq_ready, 1)
                if job >= 1 and s == LAG:
                    if job == 1:
                        dve.wait_ge(rstd_ready, 1)
                    if job % 2:
                        evac(job - 1, 0, nat[:, 1, :], rstd[:, 0, 1:2], job // 2)
                    else:
                        evac(job - 1, 1, vm[:, 1, (job // 2 - 1) * CH:(job // 2) * CH], rstd[:, 0, 1:2])
                if job in (1, 3) and s == 12:
                    natT(job // 2, kmT[:, 4 * (job // 2) + 2:4 * (job // 2) + 4, :])
                lo_slab(s, slab0(job))

            for job in range(4, 8):
                for s in range(SLABS):
                    if s == LAG:
                        if job == 4:
                            evac(3, 1, vm[:, 1, CH:], rstd[:, 0, 1:2])
                        if job == 5:
                            dve.wait_ge(rstd_ready, 2)
                        if job in (5, 6):
                            evac(job - 1, (job - 1) % 2, nat[:, 1, :], rstd_qm[:, 1:2], job - 3)
                        if job == 7:
                            gate_a(6, 0, gate)
                    if job == 7 and s == LAG + 1:
                        gate_b(0, gate)
                    if job == 7 and s == LAG + 2:
                        gate_c(0, 0, gate)
                        y_mem(0, 6)
                    if job in (6, 7) and s == 4:
                        rinv_of_mem(job - 6)
                    if job in (5, 6) and s == 12:
                        natT(job - 3, qT[:, 2:4, :])
                    if job in (6, 7) and s == 2:
                        max_mem(job - 6)
                    if job in (6, 7) and s == 11:
                        pT_out(job - 6)
                    if job == 7 and s == 14:
                        yT_out(0, X[2:4])
                    if job == 4 and s == 8:
                        dve.wait_ge(const_landed, 32)
                        nc.vector.tensor_scalar(gsub[:], gsub[:], 1.0 - LAM_INIT, None, ALU.mult).then_inc(lam_step, 1)
                        dve.wait_ge(lam_step, 5)
                    lo_slab(s, slab0(job))

            def x_job(job, steps):
                for s in range(SLABS):
                    if s in steps:
                        steps[s]()
                    lo_slab(s, slab0(job))

            def finish_steps(slot, job, y, sub):
                def last():
                    gate_c(slot, 1, gate, sub)
                    y()
                return {LAG: lambda: gate_a(job - 1, slot, gate), LAG + 1: lambda: gate_b(slot, gate),
                        LAG + 2: last, 15: lambda: yT_out(slot, X[0:2])}

            def rest_of_group(g):
                x_job(diff_job(g, 1), {LAG: lambda: evac(diff_job(g, 0), 0, nat[:, 1, :], rstd_q[:, 1:2], g * 2 + 4),
                                       12: lambda: natT(g * 2 + 4, qT[:, 2:4, :])})
                x_job(diff_job(g, 2), {LAG: lambda: evac(diff_job(g, 1), 1, nat[:, 1, :], rstd[:, 1, 1:2], g * 2 + 5),
                                       12: lambda: natT(g * 2 + 5, kT[:, 2:4, :])})
                x_job(diff_job(g, 3), {2: lambda: max_diff(g), LAG: lambda: combine(g),
                                       LAG + 1: lambda: evac(diff_job(g, 2), 0, v[:, 1, :], rstd[:, 1, 1:2]),
                                       12: lambda: pT_out(g + 2)})

            x_job(J_DIFF, finish_steps(1, J_DIFF, lambda: y_mem(1, J_DIFF - 1), None))
            with dve.Fori(0, 3) as g:
                rest_of_group(g)
                job = diff_job(g, 4)
                x_job(job, finish_steps(g + 2, job, lambda: y_diff(g, job - 1), g))
            rest_of_group(3)

            def aT_out(c):
                dve.wait_ge(dft_pos_done, c + 1)
                for b in (2, 3):
                    nc.vector.tensor_copy(aT[:, b, 0, :], X[b][:, 0:SEQ])
                    ins = nc.vector.tensor_scalar(aT[:, b, 1, :], X[b][:, SEQ:], -1.0, None, ALU.mult)
                ins.then_inc(aT_dve, 1)

            def fT_out(c):
                dve.wait_ge(fT_hi_ready, c + 1)
                for i in range(2):
                    k = slice(4 * c + 2 * i, 4 * c + 2 * i + 2)
                    ins = nc.vector.tensor_tensor(fT_lo[:, k, :], X[i][:].rearrange("p (b n) -> p b n", b=2),
                                                  fT_hi[:, k, :].bitcast(f32), ALU.subtract)
                ins.then_inc(fT_lo_ready, 1)

            x_job(24, finish_steps(5, 24, lambda: y_diff(3, 23), 3))
            x_job(25, {LAG: lambda: evac(24, 0, u[:, 0, 1, :], rstd[:, 1, 1:2]), 12: lambda: aT_out(0)})
            x_job(26, {3: lambda: fT_out(0), LAG: lambda: evac(25, 1, u[:, 1, 1, :], rstd[:, 1, 1:2]),
                       12: lambda: aT_out(1)})
            x_job(27, {3: lambda: fT_out(1), LAG: lambda: gate_a(26, 6, gate), LAG + 1: lambda: gate_b(6, gate),
                       LAG + 2: lambda: gate_c(6, 0, gate)})
            for c in range(2):
                for s in range(F_SLABS):
                    if c == 1 and s == 1:
                        gate_a(27, 7, gate1)
                    if c == 1 and s == 2:
                        gate_b(7, gate1)
                    if c == 1 and s == 3:
                        gate_c(7, 1, gate1)
                    lo_slab(s, N_WF + c * F_SLABS)

            def y_fourier(c, buf):
                dve.wait_ge(slab_used, N_WF + (c + 1) * F_SLABS)
                dve.wait_ge(evac_dve, J_ZF + c + 1)
                for t in range(T):
                    ins = nc.vector.tensor_tensor(buf[:, t, :], acc[c][:, t, :], buf[:, t, :], ALU.mult)
                    ins.then_inc((gate_step, y_ready)[t], 1)

            def residual(n, parity):
                dve.wait_ge(slab_used, n * SLABS + (N_OUT + SLABS))
                for t in range(T):
                    ins = nc.vector.tensor_tensor(acc_out[:, t, ds(n * CH, CH)], acc[parity][:, t, :],
                                                  acc_out[:, t, ds(n * CH, CH)], ALU.add)
                    ins.then_inc(summed_out, 1)

            def out_job(n, steps):
                for s in range(SLABS):
                    if s in steps:
                        steps[s]()
                    lo_slab(s, n * SLABS + N_OUT)

            out_job(0, {1: lambda: y_fourier(0, gate), LAG: lambda: y_fourier(1, gate1),
                        8: lambda: yT_out(6, X[0:2]), 13: lambda: yT_out(7, X[2:4])})
            dve.wait_ge(resid_landed, 64)
            out_job(1, {LAG: lambda: residual(0, 0)})
            with dve.Fori(1, OUT_JOBS // 2) as i:
                for parity in range(2):
                    out_job(i * 2 + parity, {LAG: lambda: residual(i * 2 + (parity - 1), 1 - parity)})
            residual(OUT_JOBS - 1, 1)
            dve.wait_ge(squared_out, 2 * OUT_JOBS)
            nc.vector.tensor_reduce(ms_f[:], ssq_f[:], AX.X, ALU.add).then_inc(ssq_f_ready, 1)
            dve.wait_ge(rstd_f_ready, 1)
            for t in range(T):
                dve.wait_ge(scaled_out, 2 * (OUT_JOBS - 1) + t + 1)
                nc.vector.tensor_scalar(acc_out[:, t, 0:D // 2], acc_out[:, t, 0:D // 2], rstd_f[:, t:t + 1], None,
                                        ALU.mult).then_inc(dve_done_out, 1)

        @block.gpsimd
        def _(pool):
            steps = [0]

            def chain(ins):
                steps[0] += 1
                ins.then_inc(pool_step, 1)
                pool.wait_ge(pool_step, steps[0])

            nc.gpsimd.memset(ident[:], 0.0).then_inc(ident_ready, 1)
            chain(nc.gpsimd.memset(half[:], -0.5))
            chain(nc.gpsimd.memset(eps[:], EPS))
            pool.wait_ge(ident_ready, 1)
            nc.gpsimd.affine_select(out=ident[:], in_=ident[:], compare_op=ALU.not_equal, fill=1.0, base=0,
                                    pattern=[[-1, P]], channel_multiplier=1).then_inc(ident_ready, 1)
            for which in range(2):
                pool.wait_ge(ssq_ready, which + 1)
                chain(nc.gpsimd.tensor_scalar(ms[:, which, :], ms[:, which, :], 1.0 / D, EPS, ALU.mult, ALU.add))
                ins = nc.gpsimd.tensor_tensor(rstd[:, which, :], ms[:, which, :], half[:, 0:T], ALU.pow)
                if which == 0:
                    ins.then_inc(rstd_ready, 1)
                else:
                    chain(ins)
                    nc.gpsimd.tensor_scalar(rstd_neg[:], rstd[:, 1, :], -1.0, None, ALU.mult)
                    nc.gpsimd.tensor_scalar(rstd_q[:], rstd[:, 1, :], DIFF_SCALE, None, ALU.mult)
                    nc.gpsimd.tensor_scalar(rstd_qm[:], rstd[:, 1, :], MEM_SCALE, None,
                                            ALU.mult).then_inc(rstd_ready, 1)
            pool.wait_ge(slab_used, 4 * SLABS)
            pool.dma_start(dist[:], dist_c.rearrange("(t p) n -> p t n", p=P)).then_inc(const_landed, 16)
            pool.dma_start(gsub[:], bass.AP(g_subln.tensor, g_subln.offset, [[0, P], [1, HD]])
                           ).then_inc(const_landed, 16)
            with pool.Fori(0, 4) as g:
                pool.wait_ge(ssq_o_ready, g + 1)
                nc.gpsimd.tensor_tensor(ssq_o[:], ssq_o[:], eps[:], ALU.add).then_inc(gsub_pool, 1)
                pool.wait_ge(gsub_pool, g + 1)
                nc.gpsimd.tensor_tensor(rstd_o[:], ssq_o[:], half[:, 0:4].rearrange("p (h t) -> p h t", h=2),
                                        ALU.pow).then_inc(rstd_o_ready, 1)
            pool.wait_ge(slab_used, N_WF)
            for c in range(4):
                cols = slice(c * (D // 4), (c + 1) * (D // 4))
                pool.dma_start(acc_out[:, :, cols], x[:, cols].rearrange("(t p) n -> p t n", p=P)
                               ).then_inc(resid_landed, 16)
            pool.dma_start(g_fin[:], bass.AP(g_final.tensor, g_final.offset, [[0, P], [1, D]])
                           ).then_inc(gfin_landed, 16)
            pool.wait_ge(gfin_landed, 16)
            with pool.Fori(0, OUT_JOBS) as n:
                for t in range(T):
                    pool.wait_ge(squared_out, n * 2 + (t + 1))
                    nc.gpsimd.tensor_tensor(acc_out[:, t, ds(n * CH, CH)], acc_out[:, t, ds(n * CH, CH)],
                                            g_fin[:, ds(n * CH, CH)], ALU.mult).then_inc(scaled_out, 1)
            pool.wait_ge(ssq_f_ready, 1)
            chain(nc.gpsimd.tensor_scalar(ms_f[:], ms_f[:], 1.0 / D, EPS, ALU.mult, ALU.add))
            nc.gpsimd.tensor_tensor(rstd_f[:], ms_f[:], half[:, 0:T], ALU.pow).then_inc(rstd_f_ready, 1)


_INS = ['x', 'mem', 'g_in', 'w_in', 'g_mem', 'w_mem_k', 'w_mem_v', 'lam_q1', 'lam_k1', 'lam_q2', 'lam_k2',
        'g_subln', 'w_fourier', 'w_out', 'g_final']
_FLAT = {'x', 'mem', 'w_in', 'w_mem_k', 'w_mem_v', 'w_fourier', 'w_out'}


def _constants():
    i = np.arange(SEQ, dtype=np.int64)
    dist = np.abs(i[:, None] - i[None, :]).astype(np.float32)
    slopes = np.array([[-2.0 ** -(h + 1) for h in range(8)]], dtype=np.float32)
    angle = 2.0 * np.pi * ((i[:, None] * i[None, :]) % SEQ).astype(np.float64) / SEQ
    dft = (np.concatenate([np.cos(angle), np.sin(angle)], axis=1) / 16.0).astype(np.float32)
    return {'dist': dist, 'slope': slopes, 'dft': dft}


def kernel(**inputs):
    import numpy as _np
    import concourse.bacc as _bacc
    from concourse import mybir as _mybir
    from concourse.bass_utils import run_bass_kernel_spmd as _run

    nc = _bacc.Bacc("TRN2", target_bir_lowering=False, num_devices=1)
    arrays, args = {}, []
    for name in _INS:
        a = _np.ascontiguousarray(inputs[name])
        if name in _FLAT:
            a = a.reshape(a.shape[1:])
        arrays[f"in_{name}_dram"] = a
        args.append(nc.dram_tensor(f"in_{name}_dram", a.shape, _mybir.dt.from_np(a.dtype), kind="ExternalInput").ap())
    for name, a in _constants().items():
        arrays[f"const_{name}_dram"] = a
        args.append(nc.dram_tensor(f"const_{name}_dram", a.shape, _mybir.dt.from_np(a.dtype),
                                   kind="ExternalInput").ap())
    args.append(nc.dram_tensor("out_0_dram", (SEQ, D), _mybir.dt.float32, kind="ExternalOutput").ap())
    hybrid_kernel(nc, *args)
    r = _run(nc, [arrays], core_ids=[0])
    return r.results[0]["out_0_dram"].reshape(1, SEQ, D)
```

```python
import numpy as np
from contextlib import ExitStack

import concourse.bass as bass
from concourse import mybir

P = 128
D = 4096
T = 2
SEQ = T * P
CH = 512
KT = D // P
SLAB_KT = 2
SLABS = KT // SLAB_KT
RING = 4
F_WIDTH = D // 4
F_SLABS = F_WIDTH // P // SLAB_KT
HD = 256
N_PIECES = 16
LAG = 5
EPS = 1e-6
LAM_INIT = 0.8 - 0.6
DIFF_COLS, F_COLS, M_COLS = D // 2, D // 4, D // 4
COL_Q, COL_K, COL_V, COL_Z = 0, DIFF_COLS, 2 * DIFF_COLS, 3 * DIFF_COLS
COL_U = 4 * DIFF_COLS
COL_ZF = COL_U + F_COLS
COL_QM = COL_ZF + F_COLS
COL_ZM = COL_QM + M_COLS
DIFF_SCALE = 128.0 ** -0.5
MEM_SCALE = 256.0 ** -0.5
Y_ORDER = [6, 7, 0, 1, 2, 3, 4, 5]
J_QM, J_ZM, J_DIFF, J_U, J_ZF, J_WF = 4, 6, 8, 24, 26, 28
N_WF = J_WF * SLABS
N_OUT = N_WF + 2 * F_SLABS
OUT_JOBS = D // CH
ACT_COLS = 768


def hybrid_kernel(nc, x, mem, g_in, w_in, g_mem, w_mem_k, w_mem_v, lam_q1, lam_k1, lam_q2, lam_k2,
                  g_subln, w_fourier, w_out, g_final, dist_c, slope_c, dft_c, out):
    f32, f32r = mybir.dt.float32, mybir.dt.float32r
    ALU, ACT, AX = mybir.AluOpType, mybir.ActivationFunctionType, mybir.AxisListType
    ds = bass.ds
    ctx = ExitStack()
    with ctx:
        KB = 1024

        def at(name, shape, dt, offset):
            return nc.alloc_sbuf_tensor_at(name, shape, dt, offset=offset)

        BASE = -(-nc.sbuf_base // 32) * 32
        A, B = BASE, BASE + 64 * KB
        RAW, HI, LO = BASE + 128 * KB, BASE + 144 * KB, BASE + 160 * KB
        W = BASE + 176 * KB
        SMALL = W + 28 * KB
        OV_HI, OV_LO = B + 24 * KB, B + 56 * KB

        xT_hi = at("xT_hi", [P, KT, SEQ], f32r, A)
        xT_lo = at("xT_lo", [P, KT, SEQ], f32r, A + 32 * KB)
        mT_hi = at("mT_hi", [P, KT, SEQ], f32r, B)
        mT_lo = at("mT_lo", [P, KT, SEQ], f32r, B + 32 * KB)
        yT_hi = at("yT_hi", [P, KT, SEQ], f32r, B)
        yT_lo = at("yT_lo", [P, KT, SEQ], f32r, B + 32 * KB)
        raw = at("raw", [P, RING, SLAB_KT, CH], f32, RAW)
        w_hi = at("w_hi", [P, RING, SLAB_KT, CH], f32r, HI)
        w_lo = at("w_lo", [P, RING, SLAB_KT, CH], f32r, LO)

        nat = at("nat", [P, T, CH], f32, W)
        qT = at("qT", [P, 4, SEQ], f32, W + 4 * KB)
        gate = at("gate", [P, T, CH], f32, W + 8 * KB)
        kmT = at("kmT", [P, 8, SEQ], f32, W + 12 * KB)
        vm = at("vm", [P, T, F_WIDTH], f32, W + 20 * KB)
        kT = at("kT", [P, 4, SEQ], f32, W + 12 * KB)
        v = at("v", [P, T, CH], f32, W + 16 * KB)
        lam_vecs = at("lam_vecs", [P, 4, P], f32, W)
        g_rows = at("g_rows", [KT, 2, P], f32, W + 2 * KB)
        stage = at("stage", [P, 4, T, SLAB_KT * P], f32, W + 4 * KB)
        fT_hi = at("fT_hi", [P, 8, SEQ], f32r, W + 12 * KB)
        fT_lo = at("fT_lo", [P, 8, SEQ], f32r, W + 20 * KB)
        gate1 = at("gate1", [P, T, CH], f32, W)
        dft = at("dft", [P, T, 2 * SEQ], f32, W + 4 * KB)
        probs = at("probs", [P, 2, 2, T, SEQ], f32, OV_HI)
        pT = at("pT", [P, 2, T, SEQ], f32, OV_LO)
        dist = at("dist", [P, T, SEQ], f32, OV_LO + 4 * KB)
        gsub = at("gsub", [P, HD], f32, OV_LO + 6 * KB)
        u = at("u", [P, 2, T, CH], f32, OV_HI)
        aT = at("aT", [P, 4, 2, SEQ], f32, OV_LO)
        acc_out = at("acc_out", [P, T, D], f32, A)
        g_fin = at("g_fin", [P, D], f32, A + 32 * KB)
        junk_out = at("junk_out", [P, T, CH], f32, A + 48 * KB)

        small_at = [SMALL]

        def small(name, shape):
            h = at(name, shape, f32, small_at[0])
            small_at[0] += -(-4 * int(np.prod(shape[1:])) // 32) * 32
            return h

        ident = small("ident", [P, P])
        junk = small("junk", [P, T, SEQ])
        gT = small("gT", [P, 2, KT])
        ssq = small("ssq", [P, 2, T, N_PIECES])
        ms = small("ms", [P, 2, T])
        rstd = small("rstd", [P, 2, T])
        rstd_neg = small("rstd_neg", [P, T])
        rstd_q = small("rstd_q", [P, T])
        rstd_qm = small("rstd_qm", [P, T])
        half = small("half", [P, 8])
        eps = small("eps", [P, 2, T])
        slopes = small("slopes", [P, 8])
        lam_prod = small("lam_prod", [P, 2, 1])
        lam_neg = small("lam_neg", [P, 1])
        negmax = small("negmax", [P, 2, 2, T])
        rowsum = small("rowsum", [P, 2, 2, T])
        rinv = small("rinv", [P, 2, 2, T])
        rinv_mem = small("rinv_mem", [P, 2, 2, T])
        ssq_o = small("ssq_o", [P, 2, T])
        rstd_o = small("rstd_o", [P, 2, T])
        ssq_f = small("ssq_f", [P, T, OUT_JOBS + 1])
        ms_f = small("ms_f", [P, T])
        rstd_f = small("rstd_f", [P, T])
        assert small_at[0] <= nc.sbuf_top

        acc = [ctx.enter_context(nc.psum_tensor(f"acc{i}", [P, T, CH], f32)) for i in range(2)]
        X = [ctx.enter_context(nc.psum_tensor(f"aux{i}", [P, CH], f32)) for i in range(4)]

        acc_banks = [[acc[i][:, t, :] for t in range(T)] for i in range(2)]
        wf_banks = [[X[0][:], X[1][:]], [X[2][:], X[3][:]]]

        def sem(name):
            return ctx.enter_context(nc.semaphore(name))

        raw_landed = [sem(f"raw_landed{i}") for i in range(RING)]
        hi_ready = sem("hi_ready")
        lo_ready = sem("lo_ready")
        slab_used = sem("slab_used")
        piece_landed = [sem(f"piece_landed{i}") for i in range(4)]
        piece_transposed = sem("piece_transposed")
        piece_squared = sem("piece_squared")
        piece_hi = sem("piece_hi")
        piece_lo = sem("piece_lo")
        evac_act = sem("evac_act")
        evac_dve = sem("evac_dve")
        nat_transposed = sem("nat_transposed")
        natT_act = sem("natT_act")
        natT_dve = sem("natT_dve")
        scores_done = sem("scores_done")
        max_ready = sem("max_ready")
        exp_ready = sem("exp_ready")
        probs_ready = sem("probs_ready")
        probs_transposed = sem("probs_transposed")
        pT_act = sem("pT_act")
        pT_dve = sem("pT_dve")
        pv_done = sem("pv_done")
        ssq_o_ready = sem("ssq_o_ready")
        rstd_o_ready = sem("rstd_o_ready")
        y_ready = sem("y_ready")
        y_transposed = sem("y_transposed")
        yT_hi_ready = sem("yT_hi_ready")
        yT_lo_ready = sem("yT_lo_ready")
        dft_pos_done = sem("dft_pos_done")
        aT_act = sem("aT_act")
        aT_dve = sem("aT_dve")
        dft_chan_done = sem("dft_chan_done")
        fT_hi_ready = sem("fT_hi_ready")
        fT_lo_ready = sem("fT_lo_ready")
        gains_landed = sem("gains_landed")
        small_landed = sem("small_landed")
        const_landed = sem("const_landed")
        dft_landed = sem("dft_landed")
        resid_landed = sem("resid_landed")
        ident_ready = sem("ident_ready")
        g_transposed = sem("g_transposed")
        gT_ready = sem("gT_ready")
        ssq_ready = sem("ssq_ready")
        ms_ready = sem("ms_ready")
        rstd_ready = sem("rstd_ready")
        lam_sums = sem("lam_sums")
        lam_exp = sem("lam_exp")
        squared_out = sem("squared_out")
        summed_out = sem("summed_out")
        scaled_out = sem("scaled_out")
        ssq_f_ready = sem("ssq_f_ready")
        rstd_f_ready = sem("rstd_f_ready")
        stored = sem("stored")
        act_done_out = sem("act_done_out")
        dve_done_out = sem("dve_done_out")
        pool_step = sem("pool_step")
        lam_step = sem("lam_step")
        gate_step = sem("gate_step")
        max_step = sem("max_step")
        comb_step = sem("comb_step")
        rinv_mem_ready = sem("rinv_mem_ready")
        gsub_step = sem("gsub_step")
        gsub_pool = sem("gsub_pool")
        gfin_landed = sem("gfin_landed")

        def diff_job(g, part):
            return g * 4 + (J_DIFF + part)

        def piece_of_input(i):
            c = (i % N_PIECES) * SLAB_KT * P
            return (mem if i < N_PIECES else x)[:, c:c + SLAB_KT * P].rearrange("(t p) n -> p t n", p=P)

        def piece_bank(i):
            return X[i % 4] if i < N_PIECES else X[i % 2]

        def slab0(job):
            return job * SLABS

        block = ctx.enter_context(nc.Block())

        @block.sync
        def _(sp):
            def load_slab(w, row0, col, s, n0, q0):
                if not (isinstance(n0, int) and n0 + s < RING):
                    sp.wait_ge(lo_ready, n0 + (s - RING + 1))
                src = w[row0:row0 + SLAB_KT * P, :].rearrange("(k p) n -> p k n", p=P)
                sp.dma_start(raw[:, s % RING], src[:, :, ds(col, CH)]).then_inc(raw_landed[s % RING], 16)

            def load_job(w, col, job):
                for s in range(SLABS):
                    load_slab(w, s * SLAB_KT * P, col, s, slab0(job), 4 * job)

            for i in range(4):
                sp.dma_start(stage[:, i], piece_of_input(i)).then_inc(piece_landed[i], 16)
                if i >= 1:
                    load_slab(w_mem_k, (i - 1) * SLAB_KT * P, 0, i - 1, 0, 0)
            for s in range(3, SLABS):
                load_slab(w_mem_k, s * SLAB_KT * P, 0, s, 0, 0)
            for j in range(1, 4):
                load_job((w_mem_k, w_mem_v)[j % 2], (j // 2) * CH, j)
            for j, col in ((4, COL_QM), (5, COL_QM + CH), (6, COL_ZM), (7, COL_ZM + CH)):
                load_job(w_in, col, j)
            with sp.Fori(0, 4) as g:
                for part, col in enumerate((COL_Q, COL_K, COL_V, COL_Z)):
                    load_job(w_in, g * CH + col, diff_job(g, part))
            sp.wait_ge(scores_done, 6)
            sp.dma_start(dft[:], dft_c.rearrange("(t p) n -> p t n", p=P)).then_inc(dft_landed, 16)
            for j, col in ((24, COL_U), (25, COL_U + CH), (26, COL_ZF), (27, COL_ZF + CH)):
                load_job(w_in, col, j)
            for c in range(2):
                for s in range(F_SLABS):
                    n0 = N_WF + c * F_SLABS
                    load_slab(w_fourier, s * SLAB_KT * P, c * CH, s, n0, n0 // RING)
            with sp.Fori(0, OUT_JOBS) as n:
                for s in range(SLABS):
                    row = (Y_ORDER[s // 2] * 4 + (s % 2) * SLAB_KT) * P
                    col = n * CH if row else n * SLABS * (CH // SLABS)
                    load_slab(w_out, row, col, s, n * SLABS + N_OUT, 0)
            for t in range(T):
                for c, cols in enumerate((slice(D - CH, D), slice(2 * ACT_COLS, D - CH))):
                    sp.wait_ge(dve_done_out, 2 * t + c + 1)
                    sp.dma_start(out[t * P:(t + 1) * P, cols], acc_out[:, t, cols]).then_inc(stored, 16)
            sp.wait_ge(stored, 16 * 8)

        @block.tensor
        def _(pe):
            def slab(s, n0, src_hi, src_lo, banks, last):
                pe.wait_ge(lo_ready, n0 + (s + 1))
                r = s % RING
                for k in range(SLAB_KT):
                    kt = s * SLAB_KT + k
                    for t in range(T):
                        o = banks[t]
                        a_hi = src_hi[:, kt, t * P:(t + 1) * P]
                        a_lo = src_lo[:, kt, t * P:(t + 1) * P]
                        end = last and k == SLAB_KT - 1
                        nc.tensor.matmul(o, a_hi, w_hi[:, r, k, :], start=(kt == 0), stop=False)
                        nc.tensor.matmul(o, a_hi, w_lo[:, r, k, :], start=False, stop=False)
                        ins = nc.tensor.matmul(o, a_lo, w_hi[:, r, k, :], start=False, stop=end)
                ins.then_inc(slab_used, 1)

            def bank_free(job):
                pe.wait_ge(evac_act, job - 1)
                pe.wait_ge(evac_dve, job - 1)

            def transposes(banks, src, blocks, block0=0):
                for b in range(blocks):
                    for t in range(T):
                        o = (b % 2) * SEQ + t * P
                        ins = nc.tensor.transpose(banks[b // 2][:, o:o + P],
                                                  src[:, t, b * P:(b + 1) * P], ident[:])
                return ins

            def transpose_nat(use, job):
                pe.wait_ge(evac_act, job + 1)
                pe.wait_ge(evac_dve, job + 1)
                transposes(X[2:4], nat, 4).then_inc(nat_transposed, 1)

            def transpose_y(slot, src, banks):
                pe.wait_ge(y_ready, slot + 1)
                transposes(banks, src, 4).then_inc(y_transposed, 1)

            def transpose_probs(use, first_map_stride):
                pe.wait_ge(probs_ready, use + 1)
                for h in range(2):
                    for kt in range(T):
                        for t in range(T):
                            ins = nc.tensor.transpose(X[h][:, kt * SEQ + t * P:kt * SEQ + (t + 1) * P],
                                                      probs[:, h, 0, t, kt * P:(kt + 1) * P], ident[:])
                ins.then_inc(probs_transposed, 1)

            def times_v(use, v_of_head):
                pe.wait_ge(pT_act, use + 1)
                pe.wait_ge(pT_dve, use + 1)
                for h in range(2):
                    for t in range(T):
                        for kt in range(T):
                            ins = nc.tensor.matmul(X[2 + h][:, t * HD:(t + 1) * HD],
                                                   pT[:, h, kt, t * P:(t + 1) * P], v_of_head(h, kt),
                                                   start=(kt == 0), stop=(kt == T - 1))
                ins.then_inc(pv_done, 1)

            pe.wait_ge(ident_ready, 2)
            pe.wait_ge(gains_landed, 16 * 2)
            for i in range(2):
                ins = nc.tensor.transpose(X[0][:, i * KT:(i + 1) * KT], g_rows[:, i, :], ident[0:KT, 0:KT])
            ins.then_inc(g_transposed, 1)

            def transpose_piece(i):
                pe.wait_ge(piece_landed[i % 4], 16 * (i // 4 + 1))
                if i == 0:
                    pe.wait_ge(gT_ready, 1)
                if i >= 4:
                    pe.wait_ge(piece_lo, i - 3 if i < N_PIECES else i - 1)
                transposes([piece_bank(i)], stage[:, i % 4], 2).then_inc(piece_transposed, 1)

            transpose_piece(0)
            transpose_piece(1)
            for n in range(4 * SLABS):
                job, s = n // SLABS, n % SLABS
                if n + 2 < N_PIECES:
                    transpose_piece(n + 2)
                if n >= SLABS and n % 2 == 0 and n // 2 + 8 < 2 * N_PIECES:
                    transpose_piece(n // 2 + 8)
                if job in (1, 3) and s == 7:
                    pe.wait_ge(piece_lo, N_PIECES)
                    if job == 3:
                        pe.wait_ge(natT_act, 1)
                        pe.wait_ge(natT_dve, 1)
                    transpose_nat(job // 2, job - 1)
                if n < N_PIECES:
                    pe.wait_ge(piece_lo, n + 1)
                if s == 0 and job >= 2:
                    bank_free(job)
                slab(s, slab0(job), mT_hi, mT_lo, acc_banks[job % 2], s == SLABS - 1)

            def scores_mem(j):
                if j == 0:
                    pe.wait_ge(piece_lo, 2 * N_PIECES)
                else:
                    pe.wait_ge(pT_act, j)
                    pe.wait_ge(pT_dve, j)
                pe.wait_ge(natT_act, 3 + j)
                pe.wait_ge(natT_dve, 3 + j)
                for h in range(2):
                    for t in range(T):
                        for d in range(2):
                            ins = nc.tensor.matmul(X[h][:, t * SEQ:(t + 1) * SEQ],
                                                   qT[:, 2 * h + d, t * P:(t + 1) * P],
                                                   kmT[:, 4 * j + 2 * h + d, :], start=(d == 0), stop=(d == 1))
                ins.then_inc(scores_done, 1)

            def mem_v(j):
                return lambda h, kt: vm[:, kt, (2 * j + h) * HD:(2 * j + h + 1) * HD]

            pe.wait_ge(piece_lo, 2 * N_PIECES)
            for job in range(4, 8):
                bank_free(job)
                for s in range(SLABS):
                    if job in (5, 6) and s == 7:
                        pe.wait_ge(natT_act, job - 3)
                        pe.wait_ge(natT_dve, job - 3)
                        transpose_nat(job - 3, job - 1)
                    if job in (5, 6) and s == 13:
                        scores_mem(job - 5)
                    if job in (6, 7) and s == 6:
                        transpose_probs(job - 6, 1)
                    if job == 6 and s == 14:
                        pe.wait_ge(evac_act, 4)
                        pe.wait_ge(evac_dve, 4)
                        times_v(0, mem_v(0))
                    if job == 7 and s == 9:
                        transpose_y(0, gate, X[2:4])
                    if job == 7 and s == 15:
                        pe.wait_ge(yT_lo_ready, 1)
                        times_v(1, mem_v(1))
                    slab(s, slab0(job), xT_hi, xT_lo, acc_banks[job % 2], s == SLABS - 1)

            def x_job(job, parity, steps):
                bank_free(job)
                for s in range(SLABS):
                    if s in steps:
                        steps[s]()
                    slab(s, slab0(job), xT_hi, xT_lo, acc_banks[parity], s == SLABS - 1)

            def finish_step(slot):
                return {13: lambda: (pe.wait_ge(pT_act, slot + 1), pe.wait_ge(pT_dve, slot + 1),
                                     transpose_y(slot, gate, X[0:2]))}

            def scores_diff(g):
                pe.wait_ge(natT_act, g * 2 + 6)
                pe.wait_ge(natT_dve, g * 2 + 6)
                pe.wait_ge(yT_lo_ready, g + 2)
                for h in range(2):
                    for c in range(2):
                        for t in range(T):
                            b = 2 * h + c
                            ins = nc.tensor.matmul(X[b][:, t * SEQ:(t + 1) * SEQ],
                                                   qT[:, b, t * P:(t + 1) * P], kT[:, b, :],
                                                   start=True, stop=True)
                ins.then_inc(scores_done, 1)

            def rest_of_group(g):
                x_job(diff_job(g, 1), 1, {7: lambda: transpose_nat(g * 2 + 4, diff_job(g, 0))})

                def transpose_k():
                    pe.wait_ge(natT_act, g * 2 + 5)
                    pe.wait_ge(natT_dve, g * 2 + 5)
                    transpose_nat(g * 2 + 5, diff_job(g, 1))

                x_job(diff_job(g, 2), 0, {7: transpose_k, 13: lambda: scores_diff(g)})

                def pv():
                    pe.wait_ge(evac_act, diff_job(g, 2) + 1)
                    pe.wait_ge(evac_dve, diff_job(g, 2) + 1)
                    times_v(g + 2, lambda h, kt: v[:, kt, h * HD:(h + 1) * HD])

                x_job(diff_job(g, 3), 1, {9: lambda: transpose_probs(g + 2, 2), 15: pv})

            x_job(J_DIFF, 0, finish_step(1))
            with pe.Fori(0, 3) as g:
                rest_of_group(g)
                x_job(diff_job(g, 4), 0, finish_step(g + 2))
            rest_of_group(3)

            def dft_positions(c):
                pe.wait_ge(evac_act, J_U + c + 1)
                pe.wait_ge(evac_dve, J_U + c + 1)
                if c == 0:
                    pe.wait_ge(dft_landed, 16)
                    pe.wait_ge(yT_lo_ready, 6)
                else:
                    pe.wait_ge(fT_lo_ready, 1)
                    pe.wait_ge(aT_dve, 1)
                for b in range(4):
                    for k in range(T):
                        ins = nc.tensor.matmul(X[b][:], u[:, c, k, b * P:(b + 1) * P], dft[:, k, :],
                                               start=(k == 0), stop=(k == T - 1))
                ins.then_inc(dft_pos_done, 1)

            def dft_channels(c):
                pe.wait_ge(aT_act, c + 1)
                pe.wait_ge(aT_dve, c + 1)
                for co in range(4):
                    for i in range(4):
                        b, part = i // 2, i % 2
                        col = part * SEQ + (co % 2) * P
                        ins = nc.tensor.matmul(X[co // 2][:, (co % 2) * SEQ:(co % 2 + 1) * SEQ],
                                               dft[:, b, col:col + P], aT[:, (co // 2) * 2 + b, part, :],
                                               start=(i == 0), stop=(i == 3))
                ins.then_inc(dft_chan_done, 1)

            x_job(24, 0, finish_step(5))
            x_job(25, 1, {7: lambda: dft_positions(0), 14: lambda: dft_channels(0)})
            x_job(26, 0, {7: lambda: dft_positions(1), 14: lambda: dft_channels(1)})
            x_job(27, 1, {})
            pe.wait_ge(fT_lo_ready, 2)
            for c in range(2):
                for s in range(F_SLABS):
                    slab(s, N_WF + c * F_SLABS, fT_hi, fT_lo, wf_banks[c], s == F_SLABS - 1)

            def out_job(n, parity, first=None):
                if first is not None:
                    bank_free(J_WF + parity)
                else:
                    pe.wait_ge(summed_out, n * 2 - 2)
                for s in range(SLABS):
                    if first and s == 5:
                        transpose_y(6, gate, X[0:2])
                    if first and s == 9:
                        transpose_y(7, gate1, X[2:4])
                    if first and s % 2 == 0:
                        pe.wait_ge(yT_lo_ready, s // 2 + 1)
                    slab(s, n * SLABS + N_OUT, yT_hi, yT_lo, acc_banks[parity], s == SLABS - 1)

            out_job(0, 0, first=True)
            out_job(1, 1, first=False)
            with pe.Fori(1, OUT_JOBS // 2) as i:
                for parity in range(2):
                    out_job(i * 2 + parity, parity)

        @block.scalar
        def _(act):
            for i, src in enumerate((g_mem, g_in)):
                act.dma_start(g_rows[:, i, :], src.rearrange("a (k p) -> (a k) p", p=P)).then_inc(gains_landed, 16)
            for i, src in enumerate((lam_q1, lam_k1, lam_q2, lam_k2)):
                act.dma_start(lam_vecs[:, i, :], bass.AP(src.tensor, src.offset, [[0, P], [1, P]])
                              ).then_inc(small_landed, 16)
            act.dma_start(slopes[:], bass.AP(slope_c.tensor, slope_c.offset, [[0, P], [1, 8]])
                          ).then_inc(small_landed, 16)

            def hi_slab(s, n0, q0):
                act.wait_ge(raw_landed[s % RING], (q0 + (s // RING + 1)) * 16)
                if not (isinstance(n0, int) and n0 + s < RING):
                    act.wait_ge(slab_used, n0 + (s - RING + 1))
                nc.scalar.activation(w_hi[:, s % RING], raw[:, s % RING], ACT.Copy).then_inc(hi_ready, 1)

            def piece(i):
                which, k0 = i // N_PIECES, (i % N_PIECES) * SLAB_KT
                dst = (mT_hi, xT_hi)[which]
                act.wait_ge(piece_landed[i % 4], 16 * (i // 4 + 1))
                act.wait_ge(piece_transposed, i + 1)
                if i == 0:
                    act.wait_ge(gT_ready, 1)
                for k in range(SLAB_KT):
                    ins = nc.scalar.activation(dst[:, k0 + k, :], piece_bank(i)[:, k * SEQ:(k + 1) * SEQ], ACT.Copy,
                                               scale=gT[:, which, k0 + k:k0 + k + 1])
                ins.then_inc(piece_hi, 1)

            def piece_squares(i):
                which = i // N_PIECES
                if i:
                    act.wait_ge(piece_squared, i)
                    if 4 <= i + 3 < 2 * N_PIECES:
                        act.dma_start(stage[:, (i + 3) % 4], piece_of_input(i + 3)
                                      ).then_inc(piece_landed[(i + 3) % 4], 16)
                for t in range(T):
                    ins = nc.scalar.activation(junk[:, t, :], stage[:, i % 4, t, :], ACT.Square,
                                               accum_out=ssq[:, which, t, i % N_PIECES:i % N_PIECES + 1])
                ins.then_inc(piece_squared, 1)

            def evac(job, parity, dst, scale, nat_use=None):
                act.wait_ge(slab_used, slab0(job) + SLABS)
                if nat_use is not None:
                    act.wait_ge(nat_transposed, nat_use)
                nc.scalar.activation(dst, acc[parity][:, 0, :], ACT.Copy, scale=scale).then_inc(evac_act, 1)

            def natT(use, dst):
                act.wait_ge(nat_transposed, use + 1)
                nc.scalar.activation(dst, X[2][:], ACT.Copy).then_inc(natT_act, 1)

            def pT_out(use):
                act.wait_ge(probs_transposed, use + 1)
                nc.scalar.activation(pT[:, 0], X[0][:], ACT.Copy).then_inc(pT_act, 1)

            def exp_mem(j):
                act.wait_ge(max_ready, j + 1)
                for h in range(2):
                    for t in range(T):
                        ins = nc.scalar.activation(probs[:, h, 0, t, :], X[h][:, t * SEQ:(t + 1) * SEQ], ACT.Exp,
                                                   bias=negmax[:, h, 0, t:t + 1],
                                                   accum_out=rowsum[:, h, 0, t:t + 1])
                ins.then_inc(probs_ready, 1)

            def exp_diff(g, h):
                act.wait_ge(max_ready, g * 2 + (3 + h))
                for c in range(2):
                    for t in range(T):
                        ins = nc.scalar.activation(probs[:, h, c, t, :], probs[:, h, c, t, :], ACT.Exp,
                                                   bias=negmax[:, h, c, t:t + 1],
                                                   accum_out=rowsum[:, h, c, t:t + 1])
                ins.then_inc(exp_ready, 1)

            def gate_exp(job, parity, dst, y_before):
                act.wait_ge(slab_used, slab0(job) + SLABS)
                if not isinstance(y_before, int) or y_before:
                    act.wait_ge(y_transposed, y_before)
                for t in range(T):
                    ins = nc.scalar.activation(dst[:, t, :], acc[parity][:, t, :], ACT.Exp,
                                               scale=rstd_neg[:, t:t + 1])
                ins.then_inc(evac_act, 1)

            def yT_out(slot, banks):
                act.wait_ge(y_transposed, slot + 1)
                for i in range(2):
                    ins = nc.scalar.activation(yT_hi[:, ds(slot * 4 + 2 * i, 2), :], banks[i][:], ACT.Copy)
                ins.then_inc(yT_hi_ready, 1)

            def squares_o(g):
                act.wait_ge(pv_done, g + 3)
                for h in range(2):
                    for t in range(T):
                        ins = nc.scalar.activation(probs[:, h, 1, t, :], X[2 + h][:, t * HD:(t + 1) * HD],
                                                   ACT.Square, scale=HD ** -0.5,
                                                   accum_out=ssq_o[:, h, t:t + 1])
                ins.then_inc(ssq_o_ready, 1)

            for n in range(4 * SLABS):
                job, s = n // SLABS, n % SLABS
                i = n if n < N_PIECES else (n - LAG) // 2 + 8
                has_piece = n < N_PIECES or (n >= SLABS + LAG and (n - LAG) % 2 == 0 and i < 2 * N_PIECES)
                if has_piece:
                    piece(i)
                if n == 8:
                    act.wait_ge(lam_sums, 1)
                    nc.scalar.activation(lam_prod[:], lam_prod[:], ACT.Exp).then_inc(lam_exp, 1)
                if job >= 1 and s == LAG:
                    if job == 1:
                        act.wait_ge(rstd_ready, 1)
                    if job % 2:
                        evac(job - 1, 0, nat[:, 0, :], rstd[:, 0, 0:1], job // 2)
                    else:
                        evac(job - 1, 1, vm[:, 0, (job // 2 - 1) * CH:(job // 2) * CH], rstd[:, 0, 0:1])
                if job in (1, 3) and s == 12:
                    natT(job // 2, kmT[:, 4 * (job // 2):4 * (job // 2) + 2, :])
                hi_slab(s, slab0(job), 4 * job)
                if has_piece:
                    piece_squares(i)

            for job in range(4, 8):
                for s in range(SLABS):
                    if s == LAG:
                        if job == 4:
                            evac(3, 1, vm[:, 0, CH:], rstd[:, 0, 0:1])
                        if job == 5:
                            act.wait_ge(rstd_ready, 2)
                        if job in (5, 6):
                            evac(job - 1, (job - 1) % 2, nat[:, 0, :], rstd_qm[:, 0:1], job - 3)
                        if job == 7:
                            gate_exp(6, 0, gate, 0)
                    if job in (5, 6) and s == 12:
                        natT(job - 3, qT[:, 0:2, :])
                    if job in (6, 7) and s == 3:
                        exp_mem(job - 6)
                    if job in (6, 7) and s == 11:
                        pT_out(job - 6)
                    if job == 7 and s == 14:
                        yT_out(0, X[2:4])
                    hi_slab(s, slab0(job), 4 * job)

            def x_job(job, steps):
                for s in range(SLABS):
                    if s in steps:
                        steps[s]()
                    hi_slab(s, slab0(job), job * 4)

            def finish_steps(slot, job):
                return {LAG: lambda: gate_exp(job - 1, 1, gate, slot)}

            def rest_of_group(g):
                x_job(diff_job(g, 1), {2: lambda: yT_out(g + 1, X[0:2]),
                                       LAG: lambda: evac(diff_job(g, 0), 0, nat[:, 0, :], rstd_q[:, 0:1], g * 2 + 4),
                                       12: lambda: natT(g * 2 + 4, qT[:, 0:2, :])})
                x_job(diff_job(g, 2), {LAG: lambda: evac(diff_job(g, 1), 1, nat[:, 0, :], rstd[:, 1, 0:1], g * 2 + 5),
                                       12: lambda: natT(g * 2 + 5, kT[:, 0:2, :])})
                x_job(diff_job(g, 3), {4: lambda: exp_diff(g, 0), 5: lambda: exp_diff(g, 1),
                                       8: lambda: evac(diff_job(g, 2), 0, v[:, 0, :], rstd[:, 1, 0:1]),
                                       14: lambda: pT_out(g + 2)})

            x_job(J_DIFF, finish_steps(1, J_DIFF))
            with act.Fori(0, 3) as g:
                rest_of_group(g)
                x_job(diff_job(g, 4), {3: lambda: squares_o(g), **finish_steps(g + 2, diff_job(g, 4))})
            rest_of_group(3)

            def aT_out(c):
                act.wait_ge(dft_pos_done, c + 1)
                for b in range(2):
                    nc.scalar.activation(aT[:, b, 0, :], X[b][:, 0:SEQ], ACT.Copy)
                    ins = nc.scalar.activation(aT[:, b, 1, :], X[b][:, SEQ:], ACT.Copy, scale=-1.0)
                ins.then_inc(aT_act, 1)

            def fT_out(c):
                act.wait_ge(dft_chan_done, c + 1)
                for i in range(2):
                    ins = nc.scalar.activation(fT_hi[:, 4 * c + 2 * i:4 * c + 2 * i + 2, :], X[i][:], ACT.Copy)
                ins.then_inc(fT_hi_ready, 1)

            x_job(24, {3: lambda: squares_o(3), **finish_steps(5, 24)})
            x_job(25, {2: lambda: yT_out(5, X[0:2]), LAG: lambda: evac(24, 0, u[:, 0, 0, :], rstd[:, 1, 0:1]), 12: lambda: aT_out(0)})
            x_job(26, {3: lambda: fT_out(0), LAG: lambda: evac(25, 1, u[:, 1, 0, :], rstd[:, 1, 0:1]),
                       12: lambda: aT_out(1)})
            x_job(27, {3: lambda: fT_out(1), LAG: lambda: gate_exp(26, 0, gate, 6)})
            for c in range(2):
                for s in range(F_SLABS):
                    if c == 1 and s == 1:
                        gate_exp(27, 1, gate1, 6)
                    hi_slab(s, N_WF + c * F_SLABS, (N_WF + c * F_SLABS) // RING)

            def squares_out(n):
                for t in range(T):
                    act.wait_ge(summed_out, n * 2 + (t + 1))
                    nc.scalar.activation(junk_out[:, t, :], acc_out[:, t, ds(n * CH, CH)], ACT.Square,
                                         scale=D ** -0.5,
                                         accum_out=ssq_f[:, t, ds(n, 1)]).then_inc(squared_out, 1)

            def out_job(n, steps):
                for s in range(SLABS):
                    if s in steps:
                        steps[s]()
                    hi_slab(s, n * SLABS + N_OUT, n * 4 + N_OUT // RING)

            out_job(0, {10: lambda: yT_out(6, X[0:2]), 13: lambda: yT_out(7, X[2:4])})
            with act.Fori(1, OUT_JOBS) as n:
                out_job(n, {LAG + 1: lambda: squares_out(n - 1)})
            squares_out(OUT_JOBS - 1)
            act.wait_ge(rstd_f_ready, 1)
            act.wait_ge(scaled_out, 2 * (OUT_JOBS - 1))
            for t in range(T):
                for c in range(2):
                    cols = slice(ACT_COLS * c, ACT_COLS * (c + 1))
                    nc.scalar.activation(acc_out[:, t, cols], acc_out[:, t, cols], ACT.Copy,
                                         scale=rstd_f[:, t:t + 1]).then_inc(act_done_out, 1)
                    act.wait_ge(act_done_out, 2 * t + c + 1)
                    act.dma_start(out[t * P:(t + 1) * P, cols], acc_out[:, t, cols]).then_inc(stored, 16)

        @block.vector
        def _(dve):
            def lo_slab(s, n0):
                dve.wait_ge(hi_ready, n0 + (s + 1))
                nc.vector.tensor_tensor(w_lo[:, s % RING], raw[:, s % RING], w_hi[:, s % RING].bitcast(f32),
                                        ALU.subtract).then_inc(lo_ready, 1)

            def piece(i):
                which, k0 = i // N_PIECES, (i % N_PIECES) * SLAB_KT
                hi, lo = ((mT_hi, mT_lo), (xT_hi, xT_lo))[which]
                dve.wait_ge(piece_hi, i + 1)
                for k in range(SLAB_KT):
                    ins = nc.vector.scalar_tensor_tensor(
                        lo[:, k0 + k, :], piece_bank(i)[:, k * SEQ:(k + 1) * SEQ], gT[:, which, k0 + k:k0 + k + 1],
                        hi[:, k0 + k, :].bitcast(f32), ALU.mult, ALU.subtract)
                ins.then_inc(piece_lo, 1)

            def evac(job, parity, dst, scale, nat_use=None):
                dve.wait_ge(slab_used, slab0(job) + SLABS)
                if nat_use is not None:
                    dve.wait_ge(nat_transposed, nat_use)
                nc.vector.tensor_scalar(dst, acc[parity][:, 1, :], scale, None, ALU.mult).then_inc(evac_dve, 1)

            def natT(use, dst):
                dve.wait_ge(nat_transposed, use + 1)
                nc.vector.tensor_copy(dst, X[3][:].rearrange("p (b n) -> p b n", b=2)).then_inc(natT_dve, 1)

            def pT_out(use):
                dve.wait_ge(probs_transposed, use + 1)
                nc.vector.tensor_copy(pT[:, 1], X[1][:].rearrange("p (b n) -> p b n", b=2)).then_inc(pT_dve, 1)

            def max_mem(j):
                dve.wait_ge(scores_done, j + 1)
                for h in range(2):
                    ins = nc.vector.tensor_reduce(negmax[:, h, 0, :], X[h][:].rearrange("p (t n) -> p t n", t=T),
                                                  AX.X, ALU.max, negate=True)
                ins.then_inc(max_ready, 1)

            def max_diff(g, h):
                dve.wait_ge(scores_done, g + 3)
                for c in range(2):
                    nc.vector.scalar_tensor_tensor(
                        probs[:, h, c], dist[:], slopes[:, ds(g * 2 + h, 1)],
                        X[2 * h + c][:].rearrange("p (t n) -> p t n", t=T),
                        ALU.mult, ALU.add).then_inc(max_step, 1)
                dve.wait_ge(max_step, g * 4 + (2 * h + 2))
                nc.vector.tensor_reduce(negmax[:, h], probs[:, h], AX.X, ALU.max, negate=True).then_inc(max_ready, 1)

            def combine(g, h):
                dve.wait_ge(exp_ready, g * 2 + (h + 1))
                nc.vector.reciprocal(rinv[:, h], rowsum[:, h]).then_inc(comb_step, 1)
                dve.wait_ge(comb_step, g * 8 + (4 * h + 1))
                nc.vector.tensor_scalar(rinv[:, h, 1, :], rinv[:, h, 1, :], lam_neg[:, 0:1], None,
                                        ALU.mult).then_inc(comb_step, 1)
                dve.wait_ge(comb_step, g * 8 + (4 * h + 2))
                for t in range(T):
                    nc.vector.tensor_scalar(probs[:, h, 1, t, :], probs[:, h, 1, t, :],
                                            rinv[:, h, 1, t:t + 1], None, ALU.mult).then_inc(comb_step, 1)
                dve.wait_ge(comb_step, g * 8 + (4 * h + 4))
                for t in range(T):
                    ins = nc.vector.scalar_tensor_tensor(probs[:, h, 0, t, :], probs[:, h, 0, t, :],
                                                         rinv[:, h, 0, t:t + 1], probs[:, h, 1, t, :],
                                                         ALU.mult, ALU.add)
                if h == 1:
                    ins.then_inc(probs_ready, 1)

            def gate_a(job, use, buf):
                dve.wait_ge(evac_act, job + 1)
                nc.vector.tensor_scalar(buf[:], buf[:], 1.0, None, ALU.add).then_inc(gate_step, 1)
                dve.wait_ge(gate_step, use * 3 + 1)
                nc.vector.reciprocal(buf[:, 0, :], buf[:, 0, :]).then_inc(gate_step, 1)

            def gate_b(use, buf):
                nc.vector.reciprocal(buf[:, 1, :], buf[:, 1, :]).then_inc(gate_step, 1)

            def gate_gain(use, sub):
                if sub is not None:
                    dve.wait_ge(gate_step, use * 3 + 3)
                    for t in range(T):
                        for h in range(2):
                            g_ = gate[:, t, h * HD:(h + 1) * HD]
                            nc.vector.tensor_tensor(g_, g_, gsub[:], ALU.mult).then_inc(gsub_step, 1)

            def gate_c(use, parity, buf, sub=None):
                dve.wait_ge(gate_step, use * 3 + 3)
                if sub is not None:
                    dve.wait_ge(gsub_step, sub * 4 + 4)
                for t in range(T):
                    ins = nc.vector.scalar_tensor_tensor(buf[:, t, :], acc[parity][:, t, :], rstd[:, 1, t:t + 1],
                                                         buf[:, t, :], ALU.mult, ALU.mult)
                ins.then_inc(evac_dve, 1)

            def y_attention(job, scale):
                dve.wait_ge(evac_dve, job + 1)
                for h in range(2):
                    for t in range(T):
                        g_ = gate[:, t, h * HD:(h + 1) * HD]
                        ins = nc.vector.scalar_tensor_tensor(g_, X[2 + h][:, t * HD:(t + 1) * HD],
                                                             scale(h, t), g_, ALU.mult, ALU.mult)
                ins.then_inc(y_ready, 1)

            def rinv_of_mem(j):
                dve.wait_ge(probs_ready, j + 1)
                nc.vector.reciprocal(rinv_mem[:, j], rowsum[:, :, 0, :]).then_inc(rinv_mem_ready, 1)

            def y_mem(j, job):
                dve.wait_ge(pv_done, j + 1)
                dve.wait_ge(rinv_mem_ready, j + 1)
                y_attention(job, lambda h, t: rinv_mem[:, j, h, t:t + 1])

            def y_diff(g, job):
                dve.wait_ge(rstd_o_ready, g + 1)
                y_attention(job, lambda h, t: rstd_o[:, h, t:t + 1])

            def yT_out(slot, banks):
                dve.wait_ge(yT_hi_ready, slot + 1)
                for i in range(2):
                    ins = nc.vector.tensor_tensor(yT_lo[:, ds(slot * 4 + 2 * i, 2), :],
                                                  banks[i][:].rearrange("p (b n) -> p b n", b=2),
                                                  yT_hi[:, ds(slot * 4 + 2 * i, 2), :].bitcast(f32), ALU.subtract)
                ins.then_inc(yT_lo_ready, 1)

            dve.wait_ge(g_transposed, 1)
            nc.vector.tensor_copy(gT[:], X[0][:, 0:2 * KT].rearrange("p (a k) -> p a k", a=2)).then_inc(gT_ready, 1)

            for n in range(4 * SLABS):
                job, s = n // SLABS, n % SLABS
                if n < N_PIECES:
                    piece(n)
                i = (n - LAG) // 2 + 8
                if n >= SLABS + LAG and (n - LAG) % 2 == 0 and i < 2 * N_PIECES:
                    piece(i)
                if n == 6:
                    dve.wait_ge(small_landed, 16 * 5)
                    for i in range(2):
                        nc.vector.tensor_tensor(lam_vecs[:, 2 * i, :], lam_vecs[:, 2 * i, :],
                                                lam_vecs[:, 2 * i + 1, :], ALU.mult).then_inc(lam_step, 1)
                    dve.wait_ge(lam_step, 2)
                    nc.vector.tensor_reduce(lam_prod[:, :, 0], lam_vecs[:, 0:4:2, :], AX.X,
                                            ALU.add).then_inc(lam_sums, 1)
                if n == 10:
                    dve.wait_ge(lam_exp, 1)
                    nc.vector.tensor_tensor(lam_neg[:], lam_prod[:, 1, :], lam_prod[:, 0, :],
                                            ALU.subtract).then_inc(lam_step, 1)
                    dve.wait_ge(lam_step, 3)
                    nc.vector.tensor_scalar(lam_neg[:], lam_neg[:], -LAM_INIT, None, ALU.add).then_inc(lam_step, 1)
                if n in (SLABS + 1, 3 * SLABS + 8):
                    which = n // (2 * SLABS)
                    dve.wait_ge(piece_squared, (which + 1) * N_PIECES)
                    nc.vector.tensor_reduce(ms[:, which, :], ssq[:, which], AX.X, ALU.add).then_inc(ssq_ready, 1)
                if job >= 1 and s == LAG:
                    if job == 1:
                        dve.wait_ge(rstd_ready, 1)
                    if job % 2:
                        evac(job - 1, 0, nat[:, 1, :], rstd[:, 0, 1:2], job // 2)
                    else:
                        evac(job - 1, 1, vm[:, 1, (job // 2 - 1) * CH:(job // 2) * CH], rstd[:, 0, 1:2])
                if job in (1, 3) and s == 12:
                    natT(job // 2, kmT[:, 4 * (job // 2) + 2:4 * (job // 2) + 4, :])
                lo_slab(s, slab0(job))

            for job in range(4, 8):
                for s in range(SLABS):
                    if s == LAG:
                        if job == 4:
                            evac(3, 1, vm[:, 1, CH:], rstd[:, 0, 1:2])
                        if job == 5:
                            dve.wait_ge(rstd_ready, 2)
                        if job in (5, 6):
                            evac(job - 1, (job - 1) % 2, nat[:, 1, :], rstd_qm[:, 1:2], job - 3)
                        if job == 7:
                            gate_a(6, 0, gate)
                    if job == 7 and s == LAG + 1:
                        gate_b(0, gate)
                    if job == 7 and s == LAG + 2:
                        gate_c(0, 0, gate)
                    if job == 7 and s == LAG + 3:
                        y_mem(0, 6)
                    if job in (6, 7) and s == 4:
                        rinv_of_mem(job - 6)
                    if job in (5, 6) and s == 12:
                        natT(job - 3, qT[:, 2:4, :])
                    if job in (6, 7) and s == 2:
                        max_mem(job - 6)
                    if job in (6, 7) and s == 11:
                        pT_out(job - 6)
                    if job == 7 and s == 14:
                        yT_out(0, X[2:4])
                    if job == 4 and s == 8:
                        dve.wait_ge(const_landed, 32)
                        nc.vector.tensor_scalar(gsub[:], gsub[:], 1.0 - LAM_INIT, None, ALU.mult).then_inc(lam_step, 1)
                        dve.wait_ge(lam_step, 5)
                    lo_slab(s, slab0(job))

            def x_job(job, steps):
                for s in range(SLABS):
                    if s in steps:
                        steps[s]()
                    lo_slab(s, slab0(job))

            def finish_steps(slot, job, y, sub):
                def last():
                    gate_c(slot, 1, gate, sub)
                return {LAG: lambda: gate_a(job - 1, slot, gate), LAG + 1: lambda: gate_b(slot, gate),
                        LAG + 2: lambda: gate_gain(slot, sub), LAG + 3: last, LAG + 4: y}

            def rest_of_group(g):
                x_job(diff_job(g, 1), {2: lambda: yT_out(g + 1, X[0:2]),
                                       LAG: lambda: evac(diff_job(g, 0), 0, nat[:, 1, :], rstd_q[:, 1:2], g * 2 + 4),
                                       12: lambda: natT(g * 2 + 4, qT[:, 2:4, :])})
                x_job(diff_job(g, 2), {LAG: lambda: evac(diff_job(g, 1), 1, nat[:, 1, :], rstd[:, 1, 1:2], g * 2 + 5),
                                       12: lambda: natT(g * 2 + 5, kT[:, 2:4, :])})
                x_job(diff_job(g, 3), {2: lambda: max_diff(g, 0), 3: lambda: max_diff(g, 1),
                                       6: lambda: combine(g, 0), 7: lambda: combine(g, 1),
                                       8: lambda: evac(diff_job(g, 2), 0, v[:, 1, :], rstd[:, 1, 1:2]),
                                       14: lambda: pT_out(g + 2)})

            x_job(J_DIFF, finish_steps(1, J_DIFF, lambda: y_mem(1, J_DIFF - 1), None))
            with dve.Fori(0, 3) as g:
                rest_of_group(g)
                job = diff_job(g, 4)
                x_job(job, finish_steps(g + 2, job, lambda: y_diff(g, job - 1), g))
            rest_of_group(3)

            def aT_out(c):
                dve.wait_ge(dft_pos_done, c + 1)
                for b in (2, 3):
                    nc.vector.tensor_copy(aT[:, b, 0, :], X[b][:, 0:SEQ])
                    ins = nc.vector.tensor_scalar(aT[:, b, 1, :], X[b][:, SEQ:], -1.0, None, ALU.mult)
                ins.then_inc(aT_dve, 1)

            def fT_out(c):
                dve.wait_ge(fT_hi_ready, c + 1)
                for i in range(2):
                    k = slice(4 * c + 2 * i, 4 * c + 2 * i + 2)
                    ins = nc.vector.tensor_tensor(fT_lo[:, k, :], X[i][:].rearrange("p (b n) -> p b n", b=2),
                                                  fT_hi[:, k, :].bitcast(f32), ALU.subtract)
                ins.then_inc(fT_lo_ready, 1)

            x_job(24, finish_steps(5, 24, lambda: y_diff(3, 23), 3))
            x_job(25, {2: lambda: yT_out(5, X[0:2]), LAG: lambda: evac(24, 0, u[:, 0, 1, :], rstd[:, 1, 1:2]), 12: lambda: aT_out(0)})
            x_job(26, {3: lambda: fT_out(0), LAG: lambda: evac(25, 1, u[:, 1, 1, :], rstd[:, 1, 1:2]),
                       12: lambda: aT_out(1)})
            x_job(27, {3: lambda: fT_out(1), LAG: lambda: gate_a(26, 6, gate), LAG + 1: lambda: gate_b(6, gate),
                       LAG + 2: lambda: gate_c(6, 0, gate)})
            for c in range(2):
                for s in range(F_SLABS):
                    if c == 1 and s == 1:
                        gate_a(27, 7, gate1)
                    if c == 1 and s == 2:
                        gate_b(7, gate1)
                    if c == 1 and s == 3:
                        gate_c(7, 1, gate1)
                    lo_slab(s, N_WF + c * F_SLABS)

            def y_fourier(c, buf):
                dve.wait_ge(slab_used, N_WF + (c + 1) * F_SLABS)
                dve.wait_ge(evac_dve, J_ZF + c + 1)
                for t in range(T):
                    ins = nc.vector.tensor_tensor(buf[:, t, :], wf_banks[c][t], buf[:, t, :], ALU.mult)
                    ins.then_inc((gate_step, y_ready)[t], 1)

            def residual(n, parity):
                dve.wait_ge(slab_used, n * SLABS + (N_OUT + SLABS))
                for t in range(T):
                    ins = nc.vector.tensor_tensor(acc_out[:, t, ds(n * CH, CH)], acc[parity][:, t, :],
                                                  acc_out[:, t, ds(n * CH, CH)], ALU.add)
                    ins.then_inc(summed_out, 1)

            def out_job(n, steps):
                for s in range(SLABS):
                    if s in steps:
                        steps[s]()
                    lo_slab(s, n * SLABS + N_OUT)

            out_job(0, {1: lambda: y_fourier(0, gate), LAG: lambda: y_fourier(1, gate1),
                        10: lambda: yT_out(6, X[0:2]), 13: lambda: yT_out(7, X[2:4])})
            dve.wait_ge(resid_landed, 64)
            out_job(1, {LAG: lambda: residual(0, 0)})
            with dve.Fori(1, OUT_JOBS // 2) as i:
                for parity in range(2):
                    out_job(i * 2 + parity, {LAG: lambda: residual(i * 2 + (parity - 1), 1 - parity)})
            residual(OUT_JOBS - 1, 1)
            dve.wait_ge(squared_out, 2 * OUT_JOBS)
            nc.vector.tensor_reduce(ms_f[:], ssq_f[:], AX.X, ALU.add).then_inc(ssq_f_ready, 1)
            dve.wait_ge(rstd_f_ready, 1)
            dve.wait_ge(scaled_out, 2 * (OUT_JOBS - 1))
            for t in range(T):
                cols = slice(D - CH, D)
                nc.vector.scalar_tensor_tensor(acc_out[:, t, cols], acc_out[:, t, cols], rstd_f[:, t:t + 1],
                                               g_fin[:, cols], ALU.mult, ALU.mult).then_inc(dve_done_out, 1)
                cols = slice(2 * ACT_COLS, D - CH)
                nc.vector.tensor_scalar(acc_out[:, t, cols], acc_out[:, t, cols], rstd_f[:, t:t + 1], None,
                                        ALU.mult).then_inc(dve_done_out, 1)

        @block.gpsimd
        def _(pool):
            steps = [0]

            def chain(ins):
                steps[0] += 1
                ins.then_inc(pool_step, 1)
                pool.wait_ge(pool_step, steps[0])

            nc.gpsimd.memset(ident[:], 0.0).then_inc(ident_ready, 1)
            chain(nc.gpsimd.memset(half[:], -0.5))
            chain(nc.gpsimd.memset(eps[:], EPS))
            chain(nc.gpsimd.memset(ssq_f[:, :, OUT_JOBS:], EPS))
            pool.wait_ge(ident_ready, 1)
            nc.gpsimd.affine_select(out=ident[:], in_=ident[:], compare_op=ALU.not_equal, fill=1.0, base=0,
                                    pattern=[[-1, P]], channel_multiplier=1).then_inc(ident_ready, 1)
            for which in range(2):
                pool.wait_ge(ssq_ready, which + 1)
                chain(nc.gpsimd.tensor_scalar(ms[:, which, :], ms[:, which, :], 1.0 / D, EPS, ALU.mult, ALU.add))
                ins = nc.gpsimd.tensor_tensor(rstd[:, which, :], ms[:, which, :], half[:, 0:T], ALU.pow)
                if which == 0:
                    ins.then_inc(rstd_ready, 1)
                else:
                    chain(ins)
                    nc.gpsimd.tensor_scalar(rstd_neg[:], rstd[:, 1, :], -1.0, None, ALU.mult)
                    nc.gpsimd.tensor_scalar(rstd_q[:], rstd[:, 1, :], DIFF_SCALE, None, ALU.mult)
                    nc.gpsimd.tensor_scalar(rstd_qm[:], rstd[:, 1, :], MEM_SCALE, None,
                                            ALU.mult).then_inc(rstd_ready, 1)
            pool.wait_ge(slab_used, 4 * SLABS)
            pool.dma_start(dist[:], dist_c.rearrange("(t p) n -> p t n", p=P)).then_inc(const_landed, 16)
            pool.dma_start(gsub[:], bass.AP(g_subln.tensor, g_subln.offset, [[0, P], [1, HD]])
                           ).then_inc(const_landed, 16)
            with pool.Fori(0, 4) as g:
                pool.wait_ge(ssq_o_ready, g + 1)
                nc.gpsimd.tensor_tensor(ssq_o[:], ssq_o[:], eps[:], ALU.add).then_inc(gsub_pool, 1)
                pool.wait_ge(gsub_pool, g + 1)
                nc.gpsimd.tensor_tensor(rstd_o[:], ssq_o[:], half[:, 0:4].rearrange("p (h t) -> p h t", h=2),
                                        ALU.pow).then_inc(rstd_o_ready, 1)
            for c in range(4):
                pool.wait_ge(slab_used, N_OUT + 3 * c)
                cols = slice(c * (D // 4), (c + 1) * (D // 4))
                pool.dma_start(acc_out[:, :, cols], x[:, cols].rearrange("(t p) n -> p t n", p=P)
                               ).then_inc(resid_landed, 16)
            pool.wait_ge(slab_used, N_OUT + 12)
            pool.dma_start(g_fin[:], bass.AP(g_final.tensor, g_final.offset, [[0, P], [1, D]])
                           ).then_inc(gfin_landed, 16)
            pool.wait_ge(gfin_landed, 16)
            with pool.Fori(0, OUT_JOBS - 1) as n:
                for t in range(T):
                    pool.wait_ge(squared_out, n * 2 + (t + 1))
                    nc.gpsimd.tensor_tensor(acc_out[:, t, ds(n * CH, CH)], acc_out[:, t, ds(n * CH, CH)],
                                            g_fin[:, ds(n * CH, CH)], ALU.mult).then_inc(scaled_out, 1)
            pool.wait_ge(ssq_f_ready, 1)
            nc.gpsimd.tensor_tensor(rstd_f[:], ms_f[:], half[:, 0:T], ALU.pow).then_inc(rstd_f_ready, 1)


_INS = ['x', 'mem', 'g_in', 'w_in', 'g_mem', 'w_mem_k', 'w_mem_v', 'lam_q1', 'lam_k1', 'lam_q2', 'lam_k2',
        'g_subln', 'w_fourier', 'w_out', 'g_final']
_FLAT = {'x', 'mem', 'w_in', 'w_mem_k', 'w_mem_v', 'w_fourier', 'w_out'}


def _constants():
    i = np.arange(SEQ, dtype=np.int64)
    dist = np.abs(i[:, None] - i[None, :]).astype(np.float32)
    slopes = np.array([[-2.0 ** -(h + 1) for h in range(8)]], dtype=np.float32)
    angle = 2.0 * np.pi * ((i[:, None] * i[None, :]) % SEQ).astype(np.float64) / SEQ
    dft = (np.concatenate([np.cos(angle), np.sin(angle)], axis=1) / 16.0).astype(np.float32)
    return {'dist': dist, 'slope': slopes, 'dft': dft}


def kernel(**inputs):
    import numpy as _np
    import concourse.bacc as _bacc
    from concourse import mybir as _mybir
    from concourse.bass_utils import run_bass_kernel_spmd as _run

    nc = _bacc.Bacc("TRN2", target_bir_lowering=False, num_devices=1)
    arrays, args = {}, []
    for name in _INS:
        a = _np.ascontiguousarray(inputs[name])
        if name in _FLAT:
            a = a.reshape(a.shape[1:])
        arrays[f"in_{name}_dram"] = a
        args.append(nc.dram_tensor(f"in_{name}_dram", a.shape, _mybir.dt.from_np(a.dtype), kind="ExternalInput").ap())
    for name, a in _constants().items():
        arrays[f"const_{name}_dram"] = a
        args.append(nc.dram_tensor(f"const_{name}_dram", a.shape, _mybir.dt.from_np(a.dtype),
                                   kind="ExternalInput").ap())
    args.append(nc.dram_tensor("out_0_dram", (SEQ, D), _mybir.dt.float32, kind="ExternalOutput").ap())
    hybrid_kernel(nc, *args)
    r = _run(nc, [arrays], core_ids=[0])
    return r.results[0]["out_0_dram"].reshape(1, SEQ, D)
```

```python
import numpy as np
from contextlib import ExitStack

import concourse.bass as bass
from concourse import mybir

P = 128
D = 4096
T = 2
SEQ = T * P
CH = 512
KT = D // P
SLAB_KT = 2
SLABS = KT // SLAB_KT
RING = 4
F_WIDTH = D // 4
F_SLABS = F_WIDTH // P // SLAB_KT
HD = 256
N_PIECES = 16
LAG = 5
EPS = 1e-6
LAM_INIT = 0.8 - 0.6
DIFF_COLS, F_COLS, M_COLS = D // 2, D // 4, D // 4
COL_Q, COL_K, COL_V, COL_Z = 0, DIFF_COLS, 2 * DIFF_COLS, 3 * DIFF_COLS
COL_U = 4 * DIFF_COLS
COL_ZF = COL_U + F_COLS
COL_QM = COL_ZF + F_COLS
COL_ZM = COL_QM + M_COLS
DIFF_SCALE = 128.0 ** -0.5
MEM_SCALE = 256.0 ** -0.5
Y_ORDER = [6, 7, 0, 1, 2, 3, 4, 5]
J_QM, J_ZM, J_DIFF, J_U, J_ZF, J_WF = 4, 6, 8, 24, 26, 28
N_WF = J_WF * SLABS
N_OUT = N_WF + 2 * F_SLABS
OUT_JOBS = D // CH
ACT_COLS = 768


def hybrid_kernel(nc, x, mem, g_in, w_in, g_mem, w_mem_k, w_mem_v, lam_q1, lam_k1, lam_q2, lam_k2,
                  g_subln, w_fourier, w_out, g_final, dist_c, slope_c, dft_c, dft_half_c, out):
    f32, f32r = mybir.dt.float32, mybir.dt.float32r
    ALU, ACT, AX = mybir.AluOpType, mybir.ActivationFunctionType, mybir.AxisListType
    ds = bass.ds
    ctx = ExitStack()
    with ctx:
        KB = 1024

        def at(name, shape, dt, offset):
            return nc.alloc_sbuf_tensor_at(name, shape, dt, offset=offset)

        BASE = -(-nc.sbuf_base // 32) * 32
        A, B = BASE, BASE + 64 * KB
        RAW, HI, LO = BASE + 128 * KB, BASE + 144 * KB, BASE + 160 * KB
        W = BASE + 176 * KB
        SMALL = W + 28 * KB
        OV_HI, OV_LO = B + 24 * KB, B + 56 * KB

        xT_hi = at("xT_hi", [P, KT, SEQ], f32r, A)
        xT_lo = at("xT_lo", [P, KT, SEQ], f32r, A + 32 * KB)
        mT_hi = at("mT_hi", [P, KT, SEQ], f32r, B)
        mT_lo = at("mT_lo", [P, KT, SEQ], f32r, B + 32 * KB)
        yT_hi = at("yT_hi", [P, KT, SEQ], f32r, B)
        yT_lo = at("yT_lo", [P, KT, SEQ], f32r, B + 32 * KB)
        raw = at("raw", [P, RING, SLAB_KT, CH], f32, RAW)
        w_hi = at("w_hi", [P, RING, SLAB_KT, CH], f32r, HI)
        w_lo = at("w_lo", [P, RING, SLAB_KT, CH], f32r, LO)

        nat = at("nat", [P, T, CH], f32, W)
        qT = at("qT", [P, 4, SEQ], f32, W + 4 * KB)
        gate = at("gate", [P, T, CH], f32, W + 8 * KB)
        kmT = at("kmT", [P, 8, SEQ], f32, W + 12 * KB)
        vm = at("vm", [P, T, F_WIDTH], f32, W + 20 * KB)
        qT_hi = at("qT_hi", [P, 4, SEQ], f32r, W + 4 * KB)
        kT_hi = at("kT_hi", [P, 4, SEQ], f32r, W + 12 * KB)
        v_hi = at("v_hi", [P, T, CH], f32r, W + 16 * KB)
        qT_lo = at("qT_lo", [P, 4, SEQ], f32r, W + 20 * KB)
        kT_lo = at("kT_lo", [P, 4, SEQ], f32r, W + 24 * KB)
        v_lo = at("v_lo", [P, T, CH], f32r, W)
        lam_vecs = at("lam_vecs", [P, 4, P], f32, W)
        g_rows = at("g_rows", [KT, 2, P], f32, W + 2 * KB)
        stage = at("stage", [P, 4, T, SLAB_KT * P], f32, W + 4 * KB)
        fT_hi = at("fT_hi", [P, 8, SEQ], f32r, W + 12 * KB)
        fT_lo = at("fT_lo", [P, 8, SEQ], f32r, W + 20 * KB)
        gate1 = at("gate1", [P, T, CH], f32, W)
        dft = at("dft", [P, T, 2 * SEQ], f32, W + 4 * KB)
        probs = at("probs", [P, 2, 2, T, SEQ], f32, OV_HI)
        pT = at("pT", [P, 2, T, SEQ], f32, OV_LO)
        pT_hi = at("pT_hi", [P, 2, T, SEQ], f32r, OV_LO)
        pT_lo = at("pT_lo", [P, 2, 2, T, SEQ], f32r, OV_HI)
        dist = at("dist", [P, T, SEQ], f32, OV_LO + 4 * KB)
        gsub = at("gsub", [P, HD], f32, OV_LO + 6 * KB)
        u = at("u", [P, 2, T, CH], f32, OV_HI)
        dft_half = at("dft_half", [P, T, SEQ], f32, W)
        aT = at("aT", [P, 4, SEQ], f32, OV_LO)
        f_all = at("f_all", [P, 4, SEQ], f32, OV_LO + 4 * KB)
        acc_out = at("acc_out", [P, T, D], f32, A)
        g_fin = at("g_fin", [P, D], f32, A + 32 * KB)
        junk_out = at("junk_out", [P, T, CH], f32, A + 48 * KB)

        small_at = [SMALL]

        def small(name, shape):
            h = at(name, shape, f32, small_at[0])
            small_at[0] += -(-4 * int(np.prod(shape[1:])) // 32) * 32
            return h

        ident = small("ident", [P, P])
        junk = small("junk", [P, T, SEQ])
        gT = small("gT", [P, 2, KT])
        ssq = small("ssq", [P, 2, T, N_PIECES])
        ms = small("ms", [P, 2, T])
        rstd = small("rstd", [P, 2, T])
        rstd_neg = small("rstd_neg", [P, T])
        rstd_q = small("rstd_q", [P, T])
        rstd_qm = small("rstd_qm", [P, T])
        half = small("half", [P, 8])
        eps = small("eps", [P, 2, T])
        slopes = small("slopes", [P, 8])
        warm = small("warm", [P, 2])
        lam_prod = small("lam_prod", [P, 2, 1])
        lam_neg = small("lam_neg", [P, 1])
        negmax = small("negmax", [P, 2, 2, T])
        rowsum = small("rowsum", [P, 2, 2, T])
        rinv = small("rinv", [P, 2, 2, T])
        rinv_mem = small("rinv_mem", [P, 2, 2, T])
        ssq_o = small("ssq_o", [P, 2, T])
        rstd_o = small("rstd_o", [P, 2, T])
        ssq_f = small("ssq_f", [P, T, OUT_JOBS + 1])
        ms_f = small("ms_f", [P, T])
        rstd_f = small("rstd_f", [P, T])
        assert small_at[0] <= nc.sbuf_top

        acc = [ctx.enter_context(nc.psum_tensor(f"acc{i}", [P, T, CH], f32)) for i in range(2)]
        X = [ctx.enter_context(nc.psum_tensor(f"aux{i}", [P, CH], f32)) for i in range(4)]

        acc_banks = [[acc[i][:, t, :] for t in range(T)] for i in range(2)]
        wf_banks = [[X[0][:], X[1][:]], [X[2][:], X[3][:]]]

        def sem(name):
            return ctx.enter_context(nc.semaphore(name))

        raw_landed = [sem(f"raw_landed{i}") for i in range(RING)]
        hi_ready = sem("hi_ready")
        lo_ready = sem("lo_ready")
        slab_used = sem("slab_used")
        piece_landed = [sem(f"piece_landed{i}") for i in range(4)]
        piece_transposed = sem("piece_transposed")
        piece_squared = sem("piece_squared")
        piece_hi = sem("piece_hi")
        piece_lo = sem("piece_lo")
        evac_act = sem("evac_act")
        evac_dve = sem("evac_dve")
        nat_transposed = sem("nat_transposed")
        natT_act = sem("natT_act")
        natT_dve = sem("natT_dve")
        scores_done = sem("scores_done")
        max_ready = sem("max_ready")
        exp_ready = sem("exp_ready")
        probs_ready = sem("probs_ready")
        probs_transposed = sem("probs_transposed")
        pT_act = sem("pT_act")
        pT_dve = sem("pT_dve")
        pv_done = sem("pv_done")
        ssq_o_ready = sem("ssq_o_ready")
        rstd_o_ready = sem("rstd_o_ready")
        y_ready = sem("y_ready")
        y_transposed = sem("y_transposed")
        yT_hi_ready = sem("yT_hi_ready")
        yT_lo_ready = sem("yT_lo_ready")
        dft_pos_done = sem("dft_pos_done")
        aT_act = sem("aT_act")
        aT_dve = sem("aT_dve")
        eo_ready = sem("eo_ready")
        f_step = sem("f_step")
        dft_chan_done = sem("dft_chan_done")
        fT_hi_ready = sem("fT_hi_ready")
        fT_lo_ready = sem("fT_lo_ready")
        gains_landed = sem("gains_landed")
        small_landed = sem("small_landed")
        const_landed = sem("const_landed")
        dft_landed = sem("dft_landed")
        resid_landed = sem("resid_landed")
        ident_ready = sem("ident_ready")
        g_transposed = sem("g_transposed")
        gT_ready = sem("gT_ready")
        ssq_ready = sem("ssq_ready")
        rstd_ready = sem("rstd_ready")
        warm_ready = sem("warm_ready")
        lam_sums = sem("lam_sums")
        lam_exp = sem("lam_exp")
        squared_out = sem("squared_out")
        summed_out = sem("summed_out")
        scaled_out = sem("scaled_out")
        ssq_f_ready = sem("ssq_f_ready")
        rstd_f_ready = sem("rstd_f_ready")
        stored = sem("stored")
        act_done_out = sem("act_done_out")
        dve_done_out = sem("dve_done_out")
        pool_step = sem("pool_step")
        lam_step = sem("lam_step")
        gate_step = sem("gate_step")
        max_step = sem("max_step")
        comb_step = sem("comb_step")
        rinv_mem_ready = sem("rinv_mem_ready")
        gsub_step = sem("gsub_step")
        gsub_pool = sem("gsub_pool")
        gfin_landed = sem("gfin_landed")

        def diff_job(g, part):
            return g * 4 + (J_DIFF + part)

        def piece_of_input(i):
            c = (i % N_PIECES) * SLAB_KT * P
            return (mem if i < N_PIECES else x)[:, c:c + SLAB_KT * P].rearrange("(t p) n -> p t n", p=P)

        def piece_bank(i):
            return X[i % 4] if i < N_PIECES else X[i % 2]

        def slab0(job):
            return job * SLABS

        block = ctx.enter_context(nc.Block())

        @block.sync
        def _(sp):
            def load_slab(w, row0, col, s, n0):
                if not (isinstance(n0, int) and n0 + s < RING):
                    sp.wait_ge(lo_ready, n0 + (s - RING + 1))
                src = w[row0:row0 + SLAB_KT * P, :].rearrange("(k p) n -> p k n", p=P)
                sp.dma_start(raw[:, s % RING], src[:, :, ds(col, CH)]).then_inc(raw_landed[s % RING], 16)

            def load_job(w, col, job):
                for s in range(SLABS):
                    load_slab(w, s * SLAB_KT * P, col, s, slab0(job))

            for i in range(4):
                sp.dma_start(stage[:, i], piece_of_input(i)).then_inc(piece_landed[i], 16)
                if i >= 1:
                    load_slab(w_mem_k, (i - 1) * SLAB_KT * P, 0, i - 1, 0)
            for s in range(3, SLABS):
                load_slab(w_mem_k, s * SLAB_KT * P, 0, s, 0)
            for j in range(1, 4):
                load_job((w_mem_k, w_mem_v)[j % 2], (j // 2) * CH, j)
            for j, col in ((4, COL_QM), (5, COL_QM + CH), (6, COL_ZM), (7, COL_ZM + CH)):
                load_job(w_in, col, j)
            with sp.Fori(0, 4) as g:
                for part, col in enumerate((COL_Q, COL_K, COL_V, COL_Z)):
                    load_job(w_in, g * CH + col, diff_job(g, part))
            sp.wait_ge(scores_done, 6)
            sp.dma_start(dft[:], dft_c.rearrange("(t p) n -> p t n", p=P)).then_inc(dft_landed, 16)
            load_job(w_in, COL_U, 24)
            sp.wait_ge(pv_done, 6)
            sp.dma_start(dft_half[:], dft_half_c.rearrange("(t p) n -> p t n", p=P)).then_inc(dft_landed, 16)
            for j, col in ((25, COL_U + CH), (26, COL_ZF), (27, COL_ZF + CH)):
                load_job(w_in, col, j)
            for c in range(2):
                for s in range(F_SLABS):
                    n0 = N_WF + c * F_SLABS
                    load_slab(w_fourier, s * SLAB_KT * P, c * CH, s, n0)
            with sp.Fori(0, OUT_JOBS) as n:
                for s in range(SLABS):
                    row = (Y_ORDER[s // 2] * 4 + (s % 2) * SLAB_KT) * P
                    col = n * CH if row else n * SLABS * (CH // SLABS)
                    load_slab(w_out, row, col, s, n * SLABS + N_OUT)
            for t in range(T):
                for c, cols in enumerate((slice(D - CH, D), slice(2 * ACT_COLS, D - CH))):
                    sp.wait_ge(dve_done_out, 2 * t + c + 1)
                    sp.dma_start(out[t * P:(t + 1) * P, cols], acc_out[:, t, cols]).then_inc(stored, 16)
            sp.wait_ge(stored, 16 * 8)

        @block.tensor
        def _(pe):
            def slab(s, n0, src_hi, src_lo, banks, last):
                pe.wait_ge(lo_ready, n0 + (s + 1))
                r = s % RING
                for k in range(SLAB_KT):
                    kt = s * SLAB_KT + k
                    for t in range(T):
                        ins = product(banks[t], src_hi[:, kt, t * P:(t + 1) * P], src_lo[:, kt, t * P:(t + 1) * P],
                                      w_hi[:, r, k, :], w_lo[:, r, k, :], kt == 0, last and k == SLAB_KT - 1)
                ins.then_inc(slab_used, 1)

            def product(o, a_hi, a_lo, b_hi, b_lo, start, stop):
                nc.tensor.matmul(o, a_hi, b_hi, start=start, stop=False)
                nc.tensor.matmul(o, a_hi, b_lo, start=False, stop=False)
                return nc.tensor.matmul(o, a_lo, b_hi, start=False, stop=stop)

            def bank_free(job):
                pe.wait_ge(evac_act, job - 1)
                pe.wait_ge(evac_dve, job - 1)

            def transposes(banks, src, blocks):
                for b in range(blocks):
                    for t in range(T):
                        o = (b % 2) * SEQ + t * P
                        ins = nc.tensor.transpose(banks[b // 2][:, o:o + P],
                                                  src[:, t, b * P:(b + 1) * P], ident[:])
                return ins

            def transpose_nat(job):
                pe.wait_ge(evac_act, job + 1)
                pe.wait_ge(evac_dve, job + 1)
                transposes(X[2:4], nat, 4).then_inc(nat_transposed, 1)

            def transpose_y(slot, src, banks):
                pe.wait_ge(y_ready, slot + 1)
                transposes(banks, src, 4).then_inc(y_transposed, 1)

            def transpose_probs(use):
                pe.wait_ge(probs_ready, use + 1)
                for h in range(2):
                    for kt in range(T):
                        for t in range(T):
                            ins = nc.tensor.transpose(X[h][:, kt * SEQ + t * P:kt * SEQ + (t + 1) * P],
                                                      probs[:, h, 0, t, kt * P:(kt + 1) * P], ident[:])
                ins.then_inc(probs_transposed, 1)

            def times_v(use, v_of_head):
                pe.wait_ge(pT_act, use + 1)
                pe.wait_ge(pT_dve, use + 1)
                for h in range(2):
                    for t in range(T):
                        for kt in range(T):
                            ins = nc.tensor.matmul(X[2 + h][:, t * HD:(t + 1) * HD],
                                                   pT[:, h, kt, t * P:(t + 1) * P], v_of_head(h, kt),
                                                   start=(kt == 0), stop=(kt == T - 1))
                ins.then_inc(pv_done, 1)

            pe.wait_ge(ident_ready, 2)
            pe.wait_ge(gains_landed, 16 * 2)
            for i in range(2):
                ins = nc.tensor.transpose(X[0][:, i * KT:(i + 1) * KT], g_rows[:, i, :], ident[0:KT, 0:KT])
            ins.then_inc(g_transposed, 1)

            def transpose_piece(i):
                pe.wait_ge(piece_landed[i % 4], 16 * (i // 4 + 1))
                if i == 0:
                    pe.wait_ge(gT_ready, 1)
                if i >= 4:
                    pe.wait_ge(piece_lo, i - 3 if i < N_PIECES else i - 1)
                transposes([piece_bank(i)], stage[:, i % 4], 2).then_inc(piece_transposed, 1)

            transpose_piece(0)
            transpose_piece(1)
            for n in range(4 * SLABS):
                job, s = n // SLABS, n % SLABS
                if n + 2 < N_PIECES:
                    transpose_piece(n + 2)
                if n >= SLABS and n % 2 == 0 and n // 2 + 8 < 2 * N_PIECES:
                    transpose_piece(n // 2 + 8)
                if job in (1, 3) and s == 7:
                    pe.wait_ge(piece_lo, N_PIECES)
                    if job == 3:
                        pe.wait_ge(natT_act, 1)
                        pe.wait_ge(natT_dve, 1)
                    transpose_nat(job - 1)
                if n < N_PIECES:
                    pe.wait_ge(piece_lo, n + 1)
                if s == 0 and job >= 2:
                    bank_free(job)
                slab(s, slab0(job), mT_hi, mT_lo, acc_banks[job % 2], s == SLABS - 1)

            def scores_mem(j):
                if j == 0:
                    pe.wait_ge(piece_lo, 2 * N_PIECES)
                else:
                    pe.wait_ge(pT_act, j)
                    pe.wait_ge(pT_dve, j)
                pe.wait_ge(natT_act, 3 + j)
                pe.wait_ge(natT_dve, 3 + j)
                for h in range(2):
                    for t in range(T):
                        for d in range(2):
                            ins = nc.tensor.matmul(X[h][:, t * SEQ:(t + 1) * SEQ],
                                                   qT[:, 2 * h + d, t * P:(t + 1) * P],
                                                   kmT[:, 4 * j + 2 * h + d, :], start=(d == 0), stop=(d == 1))
                ins.then_inc(scores_done, 1)

            def mem_v(j):
                return lambda h, kt: vm[:, kt, (2 * j + h) * HD:(2 * j + h + 1) * HD]

            pe.wait_ge(piece_lo, 2 * N_PIECES)
            for job in range(4, 8):
                bank_free(job)
                for s in range(SLABS):
                    if job in (5, 6) and s == 7:
                        pe.wait_ge(natT_act, job - 3)
                        pe.wait_ge(natT_dve, job - 3)
                        transpose_nat(job - 1)
                    if job in (5, 6) and s == 13:
                        scores_mem(job - 5)
                    if job in (6, 7) and s == 6:
                        transpose_probs(job - 6)
                    if job == 6 and s == 14:
                        pe.wait_ge(evac_act, 4)
                        pe.wait_ge(evac_dve, 4)
                        times_v(0, mem_v(0))
                    if job == 7 and s == 9:
                        transpose_y(0, gate, X[2:4])
                    if job == 7 and s == 15:
                        pe.wait_ge(yT_lo_ready, 1)
                        times_v(1, mem_v(1))
                    slab(s, slab0(job), xT_hi, xT_lo, acc_banks[job % 2], s == SLABS - 1)

            def x_job(job, parity, steps):
                bank_free(job)
                for s in range(SLABS):
                    if s in steps:
                        steps[s]()
                    slab(s, slab0(job), xT_hi, xT_lo, acc_banks[parity], s == SLABS - 1)

            def finish_step(slot):
                return {13: lambda: (pe.wait_ge(pT_act, slot + 1), pe.wait_ge(pT_dve, slot + 1),
                                     transpose_y(slot, gate, X[0:2]))}

            def scores_diff(g):
                pe.wait_ge(natT_act, g * 2 + 6)
                pe.wait_ge(natT_dve, g * 2 + 6)
                pe.wait_ge(yT_lo_ready, g + 2)
                for h in range(2):
                    for c in range(2):
                        for t in range(T):
                            b = 2 * h + c
                            ins = product(X[b][:, t * SEQ:(t + 1) * SEQ],
                                          qT_hi[:, b, t * P:(t + 1) * P], qT_lo[:, b, t * P:(t + 1) * P],
                                          kT_hi[:, b, :], kT_lo[:, b, :], True, True)
                ins.then_inc(scores_done, 1)

            def rest_of_group(g):
                x_job(diff_job(g, 1), 1, {7: lambda: transpose_nat(diff_job(g, 0))})

                def transpose_k():
                    pe.wait_ge(natT_act, g * 2 + 5)
                    pe.wait_ge(natT_dve, g * 2 + 5)
                    transpose_nat(diff_job(g, 1))

                x_job(diff_job(g, 2), 0, {7: transpose_k, 13: lambda: scores_diff(g)})

                def pv():
                    pe.wait_ge(evac_act, diff_job(g, 2) + 1)
                    pe.wait_ge(evac_dve, diff_job(g, 2) + 1)
                    pe.wait_ge(pT_act, g + 3)
                    pe.wait_ge(pT_dve, g + 3)
                    for h in range(2):
                        cols = slice(h * HD, (h + 1) * HD)
                        for t in range(T):
                            q = slice(t * P, (t + 1) * P)
                            for kt in range(T):
                                ins = product(X[2 + h][:, t * HD:(t + 1) * HD],
                                              pT_hi[:, h, kt, q], pT_lo[:, h, 1, kt, q],
                                              v_hi[:, kt, cols], v_lo[:, kt, cols], kt == 0, kt == T - 1)
                    ins.then_inc(pv_done, 1)

                x_job(diff_job(g, 3), 1, {9: lambda: transpose_probs(g + 2), 15: pv})

            x_job(J_DIFF, 0, finish_step(1))
            with pe.Fori(0, 3) as g:
                rest_of_group(g)
                x_job(diff_job(g, 4), 0, finish_step(g + 2))
            rest_of_group(3)

            def dft_positions(c):
                pe.wait_ge(evac_act, J_U + c + 1)
                pe.wait_ge(evac_dve, J_U + c + 1)
                if c == 0:
                    pe.wait_ge(dft_landed, 32)
                    pe.wait_ge(yT_lo_ready, 6)
                else:
                    pe.wait_ge(eo_ready, 1)
                    pe.wait_ge(aT_dve, 1)
                for b in range(4):
                    for k in range(T):
                        ins = nc.tensor.matmul(X[b][:, 0:SEQ], u[:, c, k, b * P:(b + 1) * P], dft_half[:, k, :],
                                               start=(k == 0), stop=(k == T - 1))
                ins.then_inc(dft_pos_done, 1)

            def dft_channels(c):
                pe.wait_ge(aT_act, c + 1)
                pe.wait_ge(aT_dve, c + 1)
                for co in range(4):
                    for part, cols in enumerate((slice(0, P + 1), slice(P + 1, SEQ))):
                        for b in range(2):
                            o = (co % 2) * SEQ
                            col = part * SEQ + (co % 2) * P
                            ins = nc.tensor.matmul(X[co // 2][:, o + cols.start:o + cols.stop],
                                                   dft[:, b, col:col + P], aT[:, (co // 2) * 2 + b, cols],
                                                   start=(b == 0), stop=(b == 1))
                ins.then_inc(dft_chan_done, 1)

            x_job(24, 0, finish_step(5))
            x_job(25, 1, {7: lambda: dft_positions(0), 14: lambda: dft_channels(0)})
            x_job(26, 0, {7: lambda: dft_positions(1), 14: lambda: dft_channels(1)})
            x_job(27, 1, {})
            pe.wait_ge(fT_lo_ready, 2)
            for c in range(2):
                for s in range(F_SLABS):
                    slab(s, N_WF + c * F_SLABS, fT_hi, fT_lo, wf_banks[c], s == F_SLABS - 1)

            def out_job(n, parity, first=None):
                if first is not None:
                    bank_free(J_WF + parity)
                else:
                    pe.wait_ge(summed_out, n * 2 - 2)
                for s in range(SLABS):
                    if first and s == 5:
                        transpose_y(6, gate, X[0:2])
                    if first and s == 9:
                        transpose_y(7, gate1, X[2:4])
                    if first and s % 2 == 0:
                        pe.wait_ge(yT_lo_ready, s // 2 + 1)
                    slab(s, n * SLABS + N_OUT, yT_hi, yT_lo, acc_banks[parity], s == SLABS - 1)

            out_job(0, 0, first=True)
            out_job(1, 1, first=False)
            with pe.Fori(1, OUT_JOBS // 2) as i:
                for parity in range(2):
                    out_job(i * 2 + parity, parity)

        @block.scalar
        def _(act):
            for i, src in enumerate((g_mem, g_in)):
                act.dma_start(g_rows[:, i, :], src.rearrange("a (k p) -> (a k) p", p=P)).then_inc(gains_landed, 16)

            act.wait_ge(warm_ready, 1)
            nc.scalar.activation(warm[:, 1:2], warm[:, 0:1], ACT.Exp)

            def hi_slab(s, n0, q0):
                act.wait_ge(raw_landed[s % RING], (q0 + (s // RING + 1)) * 16)
                if not (isinstance(n0, int) and n0 + s < RING):
                    act.wait_ge(slab_used, n0 + (s - RING + 1))
                nc.scalar.activation(w_hi[:, s % RING], raw[:, s % RING], ACT.Copy).then_inc(hi_ready, 1)

            def piece(i):
                which, k0 = i // N_PIECES, (i % N_PIECES) * SLAB_KT
                dst = (mT_hi, xT_hi)[which]
                act.wait_ge(piece_landed[i % 4], 16 * (i // 4 + 1))
                act.wait_ge(piece_transposed, i + 1)
                if i == 0:
                    act.wait_ge(gT_ready, 1)
                for k in range(SLAB_KT):
                    ins = nc.scalar.activation(dst[:, k0 + k, :], piece_bank(i)[:, k * SEQ:(k + 1) * SEQ], ACT.Copy,
                                               scale=gT[:, which, k0 + k:k0 + k + 1])
                ins.then_inc(piece_hi, 1)

            def piece_squares(i):
                which = i // N_PIECES
                if i:
                    act.wait_ge(piece_squared, i)
                    if 4 <= i + 3 < 2 * N_PIECES:
                        act.dma_start(stage[:, (i + 3) % 4], piece_of_input(i + 3)
                                      ).then_inc(piece_landed[(i + 3) % 4], 16)
                for t in range(T):
                    ins = nc.scalar.activation(junk[:, t, :], stage[:, i % 4, t, :], ACT.Square,
                                               accum_out=ssq[:, which, t, i % N_PIECES:i % N_PIECES + 1])
                ins.then_inc(piece_squared, 1)

            def evac(job, parity, dst, scale, nat_use=None):
                act.wait_ge(slab_used, slab0(job) + SLABS)
                if nat_use is not None:
                    act.wait_ge(nat_transposed, nat_use)
                nc.scalar.activation(dst, acc[parity][:, 0, :], ACT.Copy, scale=scale).then_inc(evac_act, 1)

            def natT(use, dst):
                act.wait_ge(nat_transposed, use + 1)
                nc.scalar.activation(dst, X[2][:], ACT.Copy).then_inc(natT_act, 1)

            def natT_hi(use, dst):
                act.wait_ge(nat_transposed, use + 1)
                for i in range(2):
                    ins = nc.scalar.activation(dst[:, 2 * i:2 * i + 2, :], X[2 + i][:], ACT.Copy)
                ins.then_inc(natT_act, 1)

            def evac_v(g):
                act.wait_ge(slab_used, slab0(diff_job(g, 2)) + SLABS)
                for t in range(T):
                    ins = nc.scalar.activation(v_hi[:, t, :], acc[0][:, t, :], ACT.Copy, scale=rstd[:, 1, t:t + 1])
                ins.then_inc(evac_act, 1)

            def pT_hi_out(g):
                act.wait_ge(probs_transposed, g + 3)
                for h in range(2):
                    ins = nc.scalar.activation(pT_hi[:, h], X[h][:], ACT.Copy)
                ins.then_inc(pT_act, 1)

            def pT_out(use):
                act.wait_ge(probs_transposed, use + 1)
                nc.scalar.activation(pT[:, 0], X[0][:], ACT.Copy).then_inc(pT_act, 1)

            def exp_mem(j):
                act.wait_ge(max_ready, j + 1)
                for h in range(2):
                    for t in range(T):
                        ins = nc.scalar.activation(probs[:, h, 0, t, :], X[h][:, t * SEQ:(t + 1) * SEQ], ACT.Exp,
                                                   bias=negmax[:, h, 0, t:t + 1],
                                                   accum_out=rowsum[:, h, 0, t:t + 1])
                ins.then_inc(probs_ready, 1)

            def exp_diff(g, h):
                act.wait_ge(max_ready, g * 2 + (3 + h))
                for c in range(2):
                    for t in range(T):
                        ins = nc.scalar.activation(probs[:, h, c, t, :], probs[:, h, c, t, :], ACT.Exp,
                                                   bias=negmax[:, h, c, t:t + 1],
                                                   accum_out=rowsum[:, h, c, t:t + 1])
                ins.then_inc(exp_ready, 1)

            def gate_exp(job, parity, dst, y_before):
                act.wait_ge(slab_used, slab0(job) + SLABS)
                if not isinstance(y_before, int) or y_before:
                    act.wait_ge(y_transposed, y_before)
                for t in range(T):
                    ins = nc.scalar.activation(dst[:, t, :], acc[parity][:, t, :], ACT.Exp,
                                               scale=rstd_neg[:, t:t + 1])
                ins.then_inc(evac_act, 1)

            def yT_out(slot, banks):
                act.wait_ge(y_transposed, slot + 1)
                for i in range(2):
                    ins = nc.scalar.activation(yT_hi[:, ds(slot * 4 + 2 * i, 2), :], banks[i][:], ACT.Copy)
                ins.then_inc(yT_hi_ready, 1)

            def squares_o(g):
                act.wait_ge(pv_done, g + 3)
                for h in range(2):
                    for t in range(T):
                        ins = nc.scalar.activation(probs[:, h, 1, t, :], X[2 + h][:, t * HD:(t + 1) * HD],
                                                   ACT.Square, scale=HD ** -0.5,
                                                   accum_out=ssq_o[:, h, t:t + 1])
                ins.then_inc(ssq_o_ready, 1)

            for n in range(4 * SLABS):
                job, s = n // SLABS, n % SLABS
                i = n if n < N_PIECES else (n - LAG) // 2 + 8
                has_piece = n < N_PIECES or (n >= SLABS + LAG and (n - LAG) % 2 == 0 and i < 2 * N_PIECES)
                if has_piece:
                    piece(i)
                if n == 10:
                    act.wait_ge(lam_sums, 1)
                    nc.scalar.activation(lam_prod[:], lam_prod[:], ACT.Exp).then_inc(lam_exp, 1)
                if job >= 1 and s == LAG:
                    if job == 1:
                        act.wait_ge(rstd_ready, 1)
                    if job % 2:
                        evac(job - 1, 0, nat[:, 0, :], rstd[:, 0, 0:1], job // 2)
                    else:
                        evac(job - 1, 1, vm[:, 0, (job // 2 - 1) * CH:(job // 2) * CH], rstd[:, 0, 0:1])
                if job in (1, 3) and s == 12:
                    natT(job // 2, kmT[:, 4 * (job // 2):4 * (job // 2) + 2, :])
                hi_slab(s, slab0(job), 4 * job)
                if has_piece:
                    piece_squares(i)

            for job in range(4, 8):
                for s in range(SLABS):
                    if s == LAG:
                        if job == 4:
                            evac(3, 1, vm[:, 0, CH:], rstd[:, 0, 0:1])
                        if job == 5:
                            act.wait_ge(rstd_ready, 2)
                        if job in (5, 6):
                            evac(job - 1, (job - 1) % 2, nat[:, 0, :], rstd_qm[:, 0:1], job - 3)
                        if job == 7:
                            gate_exp(6, 0, gate, 0)
                    if job in (5, 6) and s == 12:
                        natT(job - 3, qT[:, 0:2, :])
                    if job in (6, 7) and s == 3:
                        exp_mem(job - 6)
                    if job in (6, 7) and s == 11:
                        pT_out(job - 6)
                    if job == 7 and s == 14:
                        yT_out(0, X[2:4])
                    hi_slab(s, slab0(job), 4 * job)

            def x_job(job, steps):
                for s in range(SLABS):
                    if s in steps:
                        steps[s]()
                    hi_slab(s, slab0(job), job * 4)

            def finish_steps(slot, job):
                return {LAG: lambda: gate_exp(job - 1, 1, gate, slot)}

            def rest_of_group(g):
                x_job(diff_job(g, 1), {2: lambda: yT_out(g + 1, X[0:2]),
                                       LAG: lambda: evac(diff_job(g, 0), 0, nat[:, 0, :], rstd_q[:, 0:1], g * 2 + 4),
                                       12: lambda: natT_hi(g * 2 + 4, qT_hi)})
                x_job(diff_job(g, 2), {LAG: lambda: evac(diff_job(g, 1), 1, nat[:, 0, :], rstd[:, 1, 0:1], g * 2 + 5),
                                       12: lambda: natT_hi(g * 2 + 5, kT_hi)})
                x_job(diff_job(g, 3), {4: lambda: exp_diff(g, 0), 5: lambda: exp_diff(g, 1),
                                       8: lambda: evac_v(g),
                                       14: lambda: pT_hi_out(g)})

            x_job(J_DIFF, finish_steps(1, J_DIFF))
            with act.Fori(0, 3) as g:
                rest_of_group(g)
                x_job(diff_job(g, 4), {3: lambda: squares_o(g), **finish_steps(g + 2, diff_job(g, 4))})
            rest_of_group(3)

            def aT_out(c):
                act.wait_ge(dft_pos_done, c + 1)
                for b in range(2):
                    ins = nc.scalar.activation(aT[:, b, :], X[b][:, 0:SEQ], ACT.Copy)
                ins.then_inc(aT_act, 1)

            def even_odd_out(c):
                act.wait_ge(dft_chan_done, c + 1)
                for i in range(2):
                    ins = nc.scalar.activation(u[:, c, i, :], X[i][:], ACT.Copy)
                ins.then_inc(eo_ready, 1)

            def fT_hi_out(c):
                act.wait_ge(f_step, 3 * c + 3)
                nc.scalar.activation(fT_hi[:, 4 * c:4 * c + 4, :], f_all[:], ACT.Copy).then_inc(fT_hi_ready, 1)

            x_job(24, {3: lambda: squares_o(3), **finish_steps(5, 24)})
            x_job(25, {2: lambda: yT_out(5, X[0:2]),
                       LAG: lambda: evac(24, 0, u[:, 0, 0, :], rstd[:, 1, 0:1]),
                       12: lambda: aT_out(0)})
            x_job(26, {3: lambda: even_odd_out(0), LAG: lambda: evac(25, 1, u[:, 1, 0, :], rstd[:, 1, 0:1]),
                       6: lambda: fT_hi_out(0), 12: lambda: aT_out(1)})
            x_job(27, {3: lambda: even_odd_out(1), LAG: lambda: gate_exp(26, 0, gate, 6), 6: lambda: fT_hi_out(1)})
            for c in range(2):
                for s in range(F_SLABS):
                    if c == 1 and s == 1:
                        gate_exp(27, 1, gate1, 6)
                    hi_slab(s, N_WF + c * F_SLABS, (N_WF + c * F_SLABS) // RING)

            def squares_out(n):
                for t in range(T):
                    act.wait_ge(summed_out, n * 2 + (t + 1))
                    nc.scalar.activation(junk_out[:, t, :], acc_out[:, t, ds(n * CH, CH)], ACT.Square,
                                         scale=D ** -0.5,
                                         accum_out=ssq_f[:, t, ds(n, 1)]).then_inc(squared_out, 1)

            def out_job(n, steps):
                for s in range(SLABS):
                    if s in steps:
                        steps[s]()
                    hi_slab(s, n * SLABS + N_OUT, n * 4 + N_OUT // RING)

            out_job(0, {10: lambda: yT_out(6, X[0:2]), 13: lambda: yT_out(7, X[2:4])})
            with act.Fori(1, OUT_JOBS) as n:
                out_job(n, {LAG + 1: lambda: squares_out(n - 1)})
            squares_out(OUT_JOBS - 1)
            act.wait_ge(rstd_f_ready, 1)
            act.wait_ge(scaled_out, 2 * (OUT_JOBS - 1))
            for t in range(T):
                for c in range(2):
                    cols = slice(ACT_COLS * c, ACT_COLS * (c + 1))
                    nc.scalar.activation(acc_out[:, t, cols], acc_out[:, t, cols], ACT.Copy,
                                         scale=rstd_f[:, t:t + 1]).then_inc(act_done_out, 1)
                    act.wait_ge(act_done_out, 2 * t + c + 1)
                    act.dma_start(out[t * P:(t + 1) * P, cols], acc_out[:, t, cols]).then_inc(stored, 16)

        @block.vector
        def _(dve):
            def lo_slab(s, n0):
                dve.wait_ge(hi_ready, n0 + (s + 1))
                nc.vector.tensor_tensor(w_lo[:, s % RING], raw[:, s % RING], w_hi[:, s % RING].bitcast(f32),
                                        ALU.subtract).then_inc(lo_ready, 1)

            def piece(i):
                which, k0 = i // N_PIECES, (i % N_PIECES) * SLAB_KT
                hi, lo = ((mT_hi, mT_lo), (xT_hi, xT_lo))[which]
                dve.wait_ge(piece_hi, i + 1)
                for k in range(SLAB_KT):
                    ins = nc.vector.scalar_tensor_tensor(
                        lo[:, k0 + k, :], piece_bank(i)[:, k * SEQ:(k + 1) * SEQ], gT[:, which, k0 + k:k0 + k + 1],
                        hi[:, k0 + k, :].bitcast(f32), ALU.mult, ALU.subtract)
                ins.then_inc(piece_lo, 1)

            def evac(job, parity, dst, scale, nat_use=None):
                dve.wait_ge(slab_used, slab0(job) + SLABS)
                if nat_use is not None:
                    dve.wait_ge(nat_transposed, nat_use)
                nc.vector.tensor_scalar(dst, acc[parity][:, 1, :], scale, None, ALU.mult).then_inc(evac_dve, 1)

            def natT(use, dst):
                dve.wait_ge(nat_transposed, use + 1)
                nc.vector.tensor_copy(dst, X[3][:].rearrange("p (b n) -> p b n", b=2)).then_inc(natT_dve, 1)

            def natT_lo(use, hi, lo):
                dve.wait_ge(natT_act, use + 1)
                for i in range(2):
                    b = slice(2 * i, 2 * i + 2)
                    ins = nc.vector.tensor_tensor(lo[:, b, :], X[2 + i][:].rearrange("p (b n) -> p b n", b=2),
                                                  hi[:, b, :].bitcast(f32), ALU.subtract)
                ins.then_inc(natT_dve, 1)

            def evac_v(g):
                dve.wait_ge(evac_act, diff_job(g, 2) + 1)
                for t in range(T):
                    ins = nc.vector.scalar_tensor_tensor(v_lo[:, t, :], acc[0][:, t, :], rstd[:, 1, t:t + 1],
                                                         v_hi[:, t, :].bitcast(f32), ALU.mult, ALU.subtract)
                ins.then_inc(evac_dve, 1)

            def pT_lo_out(g):
                dve.wait_ge(pT_act, g + 3)
                for h in range(2):
                    ins = nc.vector.tensor_tensor(pT_lo[:, h, 1], X[h][:].rearrange("p (b n) -> p b n", b=2),
                                                  pT_hi[:, h].bitcast(f32), ALU.subtract)
                ins.then_inc(pT_dve, 1)

            def pT_out(use):
                dve.wait_ge(probs_transposed, use + 1)
                nc.vector.tensor_copy(pT[:, 1], X[1][:].rearrange("p (b n) -> p b n", b=2)).then_inc(pT_dve, 1)

            def max_mem(j):
                dve.wait_ge(scores_done, j + 1)
                for h in range(2):
                    ins = nc.vector.tensor_reduce(negmax[:, h, 0, :], X[h][:].rearrange("p (t n) -> p t n", t=T),
                                                  AX.X, ALU.max, negate=True)
                ins.then_inc(max_ready, 1)

            def max_diff(g, h):
                dve.wait_ge(scores_done, g + 3)
                for c in range(2):
                    nc.vector.scalar_tensor_tensor(
                        probs[:, h, c], dist[:], slopes[:, ds(g * 2 + h, 1)],
                        X[2 * h + c][:].rearrange("p (t n) -> p t n", t=T),
                        ALU.mult, ALU.add).then_inc(max_step, 1)
                dve.wait_ge(max_step, g * 4 + (2 * h + 2))
                nc.vector.tensor_reduce(negmax[:, h], probs[:, h], AX.X, ALU.max, negate=True).then_inc(max_ready, 1)

            def combine(g, h):
                dve.wait_ge(exp_ready, g * 2 + (h + 1))
                nc.vector.reciprocal(rinv[:, h], rowsum[:, h]).then_inc(comb_step, 1)
                dve.wait_ge(comb_step, g * 8 + (4 * h + 1))
                nc.vector.tensor_scalar(rinv[:, h, 1, :], rinv[:, h, 1, :], lam_neg[:, 0:1], None,
                                        ALU.mult).then_inc(comb_step, 1)
                dve.wait_ge(comb_step, g * 8 + (4 * h + 2))
                for t in range(T):
                    nc.vector.tensor_scalar(probs[:, h, 1, t, :], probs[:, h, 1, t, :],
                                            rinv[:, h, 1, t:t + 1], None, ALU.mult).then_inc(comb_step, 1)
                dve.wait_ge(comb_step, g * 8 + (4 * h + 4))
                for t in range(T):
                    ins = nc.vector.scalar_tensor_tensor(probs[:, h, 0, t, :], probs[:, h, 0, t, :],
                                                         rinv[:, h, 0, t:t + 1], probs[:, h, 1, t, :],
                                                         ALU.mult, ALU.add)
                if h == 1:
                    ins.then_inc(probs_ready, 1)

            def gate_a(job, use, buf):
                dve.wait_ge(evac_act, job + 1)
                nc.vector.tensor_scalar(buf[:], buf[:], 1.0, None, ALU.add).then_inc(gate_step, 1)
                dve.wait_ge(gate_step, use * 3 + 1)
                nc.vector.reciprocal(buf[:, 0, :], buf[:, 0, :]).then_inc(gate_step, 1)

            def gate_b(use, buf):
                nc.vector.reciprocal(buf[:, 1, :], buf[:, 1, :]).then_inc(gate_step, 1)

            def gate_gain(use, sub):
                if sub is not None:
                    dve.wait_ge(gate_step, use * 3 + 3)
                    for t in range(T):
                        for h in range(2):
                            g_ = gate[:, t, h * HD:(h + 1) * HD]
                            nc.vector.tensor_tensor(g_, g_, gsub[:], ALU.mult).then_inc(gsub_step, 1)

            def gate_c(use, parity, buf, sub=None):
                dve.wait_ge(gate_step, use * 3 + 3)
                if sub is not None:
                    dve.wait_ge(gsub_step, sub * 4 + 4)
                for t in range(T):
                    ins = nc.vector.scalar_tensor_tensor(buf[:, t, :], acc[parity][:, t, :], rstd[:, 1, t:t + 1],
                                                         buf[:, t, :], ALU.mult, ALU.mult)
                ins.then_inc(evac_dve, 1)

            def y_attention(job, scale):
                dve.wait_ge(evac_dve, job + 1)
                for h in range(2):
                    for t in range(T):
                        g_ = gate[:, t, h * HD:(h + 1) * HD]
                        ins = nc.vector.scalar_tensor_tensor(g_, X[2 + h][:, t * HD:(t + 1) * HD],
                                                             scale(h, t), g_, ALU.mult, ALU.mult)
                ins.then_inc(y_ready, 1)

            def rinv_of_mem(j):
                dve.wait_ge(probs_ready, j + 1)
                nc.vector.reciprocal(rinv_mem[:, j], rowsum[:, :, 0, :]).then_inc(rinv_mem_ready, 1)

            def y_mem(j, job):
                dve.wait_ge(pv_done, j + 1)
                dve.wait_ge(rinv_mem_ready, j + 1)
                y_attention(job, lambda h, t: rinv_mem[:, j, h, t:t + 1])

            def y_diff(g, job):
                dve.wait_ge(rstd_o_ready, g + 1)
                y_attention(job, lambda h, t: rstd_o[:, h, t:t + 1])

            def yT_out(slot, banks):
                dve.wait_ge(yT_hi_ready, slot + 1)
                for i in range(2):
                    ins = nc.vector.tensor_tensor(yT_lo[:, ds(slot * 4 + 2 * i, 2), :],
                                                  banks[i][:].rearrange("p (b n) -> p b n", b=2),
                                                  yT_hi[:, ds(slot * 4 + 2 * i, 2), :].bitcast(f32), ALU.subtract)
                ins.then_inc(yT_lo_ready, 1)

            nc.vector.memset(warm[:], 0.0).then_inc(warm_ready, 1)
            dve.wait_ge(g_transposed, 1)
            nc.vector.tensor_copy(gT[:], X[0][:, 0:2 * KT].rearrange("p (a k) -> p a k", a=2)).then_inc(gT_ready, 1)

            for n in range(4 * SLABS):
                job, s = n // SLABS, n % SLABS
                if n < N_PIECES:
                    piece(n)
                i = (n - LAG) // 2 + 8
                if n >= SLABS + LAG and (n - LAG) % 2 == 0 and i < 2 * N_PIECES:
                    piece(i)
                if n == 7:
                    dve.wait_ge(small_landed, 16 * 5)
                    for i in range(2):
                        nc.vector.tensor_tensor(lam_vecs[:, 2 * i, :], lam_vecs[:, 2 * i, :],
                                                lam_vecs[:, 2 * i + 1, :], ALU.mult).then_inc(lam_step, 1)
                    dve.wait_ge(lam_step, 2)
                    nc.vector.tensor_reduce(lam_prod[:, :, 0], lam_vecs[:, 0:4:2, :], AX.X,
                                            ALU.add).then_inc(lam_sums, 1)
                if n == 13:
                    dve.wait_ge(lam_exp, 1)
                    nc.vector.tensor_tensor(lam_neg[:], lam_prod[:, 1, :], lam_prod[:, 0, :],
                                            ALU.subtract).then_inc(lam_step, 1)
                    dve.wait_ge(lam_step, 3)
                    nc.vector.tensor_scalar(lam_neg[:], lam_neg[:], -LAM_INIT, None, ALU.add).then_inc(lam_step, 1)
                if n in (SLABS + 1, 3 * SLABS + 8):
                    which = n // (2 * SLABS)
                    dve.wait_ge(piece_squared, (which + 1) * N_PIECES)
                    nc.vector.tensor_reduce(ms[:, which, :], ssq[:, which], AX.X, ALU.add).then_inc(ssq_ready, 1)
                if job >= 1 and s == LAG:
                    if job == 1:
                        dve.wait_ge(rstd_ready, 1)
                    if job % 2:
                        evac(job - 1, 0, nat[:, 1, :], rstd[:, 0, 1:2], job // 2)
                    else:
                        evac(job - 1, 1, vm[:, 1, (job // 2 - 1) * CH:(job // 2) * CH], rstd[:, 0, 1:2])
                if job in (1, 3) and s == 12:
                    natT(job // 2, kmT[:, 4 * (job // 2) + 2:4 * (job // 2) + 4, :])
                lo_slab(s, slab0(job))

            for job in range(4, 8):
                for s in range(SLABS):
                    if s == LAG:
                        if job == 4:
                            evac(3, 1, vm[:, 1, CH:], rstd[:, 0, 1:2])
                        if job == 5:
                            dve.wait_ge(rstd_ready, 2)
                        if job in (5, 6):
                            evac(job - 1, (job - 1) % 2, nat[:, 1, :], rstd_qm[:, 1:2], job - 3)
                        if job == 7:
                            gate_a(6, 0, gate)
                    if job == 7 and s == LAG + 1:
                        gate_b(0, gate)
                    if job == 7 and s == LAG + 2:
                        gate_c(0, 0, gate)
                    if job == 7 and s == LAG + 3:
                        y_mem(0, 6)
                    if job in (6, 7) and s == 4:
                        rinv_of_mem(job - 6)
                    if job in (5, 6) and s == 12:
                        natT(job - 3, qT[:, 2:4, :])
                    if job in (6, 7) and s == 2:
                        max_mem(job - 6)
                    if job in (6, 7) and s == 11:
                        pT_out(job - 6)
                    if job == 7 and s == 14:
                        yT_out(0, X[2:4])
                    if job == 4 and s == 8:
                        dve.wait_ge(const_landed, 32)
                        nc.vector.tensor_scalar(gsub[:], gsub[:], 1.0 - LAM_INIT, None, ALU.mult).then_inc(lam_step, 1)
                        dve.wait_ge(lam_step, 5)
                    lo_slab(s, slab0(job))

            def x_job(job, steps):
                for s in range(SLABS):
                    if s in steps:
                        steps[s]()
                    lo_slab(s, slab0(job))

            def finish_steps(slot, job, y, sub):
                def last():
                    gate_c(slot, 1, gate, sub)
                return {LAG: lambda: gate_a(job - 1, slot, gate), LAG + 1: lambda: gate_b(slot, gate),
                        LAG + 2: lambda: gate_gain(slot, sub), LAG + 3: last, LAG + 4: y}

            def rest_of_group(g):
                x_job(diff_job(g, 1), {2: lambda: yT_out(g + 1, X[0:2]),
                                       LAG: lambda: evac(diff_job(g, 0), 0, nat[:, 1, :], rstd_q[:, 1:2], g * 2 + 4),
                                       12: lambda: natT_lo(g * 2 + 4, qT_hi, qT_lo)})
                x_job(diff_job(g, 2), {LAG: lambda: evac(diff_job(g, 1), 1, nat[:, 1, :], rstd[:, 1, 1:2], g * 2 + 5),
                                       12: lambda: natT_lo(g * 2 + 5, kT_hi, kT_lo)})
                x_job(diff_job(g, 3), {2: lambda: max_diff(g, 0), 3: lambda: max_diff(g, 1),
                                       6: lambda: combine(g, 0), 7: lambda: combine(g, 1),
                                       8: lambda: evac_v(g),
                                       14: lambda: pT_lo_out(g)})

            x_job(J_DIFF, finish_steps(1, J_DIFF, lambda: y_mem(1, J_DIFF - 1), None))
            with dve.Fori(0, 3) as g:
                rest_of_group(g)
                job = diff_job(g, 4)
                x_job(job, finish_steps(g + 2, job, lambda: y_diff(g, job - 1), g))
            rest_of_group(3)

            def aT_out(c):
                dve.wait_ge(dft_pos_done, c + 1)
                for b in (2, 3):
                    ins = nc.vector.tensor_copy(aT[:, b, :], X[b][:, 0:SEQ])
                ins.then_inc(aT_dve, 1)

            def all_positions(c):
                dve.wait_ge(eo_ready, c + 1)
                if c:
                    dve.wait_ge(fT_lo_ready, c)
                eo = u[:, c].rearrange("p i (b n) -> p (i b) n", b=2)
                nc.vector.tensor_copy(f_all[:, :, 0:P + 1:P], eo[:, :, 0:P + 1:P]).then_inc(f_step, 1)
                nc.vector.tensor_tensor(f_all[:, :, 1:P], eo[:, :, 1:P], eo[:, :, P + 1:SEQ],
                                        ALU.subtract).then_inc(f_step, 1)
                nc.vector.tensor_tensor(f_all[:, :, P + 1:SEQ][:, :, ::-1], eo[:, :, 1:P], eo[:, :, P + 1:SEQ],
                                        ALU.add).then_inc(f_step, 1)

            def fT_lo_out(c):
                dve.wait_ge(fT_hi_ready, c + 1)
                nc.vector.tensor_tensor(fT_lo[:, 4 * c:4 * c + 4, :], f_all[:],
                                        fT_hi[:, 4 * c:4 * c + 4, :].bitcast(f32),
                                        ALU.subtract).then_inc(fT_lo_ready, 1)

            x_job(24, finish_steps(5, 24, lambda: y_diff(3, 23), 3))
            x_job(25, {2: lambda: yT_out(5, X[0:2]),
                       LAG: lambda: evac(24, 0, u[:, 0, 1, :], rstd[:, 1, 1:2]),
                       12: lambda: aT_out(0)})
            x_job(26, {4: lambda: all_positions(0), 7: lambda: fT_lo_out(0),
                       LAG: lambda: evac(25, 1, u[:, 1, 1, :], rstd[:, 1, 1:2]),
                       12: lambda: aT_out(1)})
            x_job(27, {4: lambda: all_positions(1), 7: lambda: fT_lo_out(1), 9: lambda: gate_a(26, 6, gate),
                       10: lambda: gate_b(6, gate), 11: lambda: gate_c(6, 0, gate)})
            for c in range(2):
                for s in range(F_SLABS):
                    if c == 1 and s == 1:
                        gate_a(27, 7, gate1)
                    if c == 1 and s == 2:
                        gate_b(7, gate1)
                    if c == 1 and s == 3:
                        gate_c(7, 1, gate1)
                    lo_slab(s, N_WF + c * F_SLABS)

            def y_fourier(c, buf):
                dve.wait_ge(slab_used, N_WF + (c + 1) * F_SLABS)
                dve.wait_ge(evac_dve, J_ZF + c + 1)
                for t in range(T):
                    ins = nc.vector.tensor_tensor(buf[:, t, :], wf_banks[c][t], buf[:, t, :], ALU.mult)
                    ins.then_inc((gate_step, y_ready)[t], 1)

            def residual(n, parity):
                dve.wait_ge(slab_used, n * SLABS + (N_OUT + SLABS))
                for t in range(T):
                    ins = nc.vector.tensor_tensor(acc_out[:, t, ds(n * CH, CH)], acc[parity][:, t, :],
                                                  acc_out[:, t, ds(n * CH, CH)], ALU.add)
                    ins.then_inc(summed_out, 1)

            def out_job(n, steps):
                for s in range(SLABS):
                    if s in steps:
                        steps[s]()
                    lo_slab(s, n * SLABS + N_OUT)

            out_job(0, {1: lambda: y_fourier(0, gate), LAG: lambda: y_fourier(1, gate1),
                        10: lambda: yT_out(6, X[0:2]), 13: lambda: yT_out(7, X[2:4])})
            dve.wait_ge(resid_landed, 64)
            out_job(1, {LAG: lambda: residual(0, 0)})
            with dve.Fori(1, OUT_JOBS // 2) as i:
                for parity in range(2):
                    out_job(i * 2 + parity, {LAG: lambda: residual(i * 2 + (parity - 1), 1 - parity)})
            residual(OUT_JOBS - 1, 1)
            dve.wait_ge(squared_out, 2 * OUT_JOBS)
            nc.vector.tensor_reduce(ms_f[:], ssq_f[:], AX.X, ALU.add).then_inc(ssq_f_ready, 1)
            dve.wait_ge(rstd_f_ready, 1)
            dve.wait_ge(scaled_out, 2 * (OUT_JOBS - 1))
            for t in range(T):
                cols = slice(D - CH, D)
                nc.vector.scalar_tensor_tensor(acc_out[:, t, cols], acc_out[:, t, cols], rstd_f[:, t:t + 1],
                                               g_fin[:, cols], ALU.mult, ALU.mult).then_inc(dve_done_out, 1)
                cols = slice(2 * ACT_COLS, D - CH)
                nc.vector.tensor_scalar(acc_out[:, t, cols], acc_out[:, t, cols], rstd_f[:, t:t + 1], None,
                                        ALU.mult).then_inc(dve_done_out, 1)

        @block.gpsimd
        def _(pool):
            steps = [0]

            def chain(ins):
                steps[0] += 1
                ins.then_inc(pool_step, 1)
                pool.wait_ge(pool_step, steps[0])

            nc.gpsimd.memset(ident[:], 0.0).then_inc(ident_ready, 1)
            pool.wait_ge(ident_ready, 1)
            nc.gpsimd.affine_select(out=ident[:], in_=ident[:], compare_op=ALU.not_equal, fill=1.0, base=0,
                                    pattern=[[-1, P]], channel_multiplier=1).then_inc(ident_ready, 1)
            chain(nc.gpsimd.memset(half[:], -0.5))
            chain(nc.gpsimd.memset(eps[:], EPS))
            chain(nc.gpsimd.memset(ssq_f[:, :, OUT_JOBS:], EPS))
            for i, src in enumerate((lam_q1, lam_k1, lam_q2, lam_k2)):
                pool.dma_start(lam_vecs[:, i, :], bass.AP(src.tensor, src.offset, [[0, P], [1, P]])
                               ).then_inc(small_landed, 16)
            pool.dma_start(slopes[:], bass.AP(slope_c.tensor, slope_c.offset, [[0, P], [1, 8]])
                           ).then_inc(small_landed, 16)
            for which in range(2):
                pool.wait_ge(ssq_ready, which + 1)
                chain(nc.gpsimd.tensor_scalar(ms[:, which, :], ms[:, which, :], 1.0 / D, EPS, ALU.mult, ALU.add))
                ins = nc.gpsimd.tensor_tensor(rstd[:, which, :], ms[:, which, :], half[:, 0:T], ALU.pow)
                if which == 0:
                    ins.then_inc(rstd_ready, 1)
                else:
                    chain(ins)
                    nc.gpsimd.tensor_scalar(rstd_neg[:], rstd[:, 1, :], -1.0, None, ALU.mult)
                    nc.gpsimd.tensor_scalar(rstd_q[:], rstd[:, 1, :], DIFF_SCALE, None, ALU.mult)
                    nc.gpsimd.tensor_scalar(rstd_qm[:], rstd[:, 1, :], MEM_SCALE, None,
                                            ALU.mult).then_inc(rstd_ready, 1)
            pool.wait_ge(slab_used, 4 * SLABS)
            pool.dma_start(dist[:], dist_c.rearrange("(t p) n -> p t n", p=P)).then_inc(const_landed, 16)
            pool.dma_start(gsub[:], bass.AP(g_subln.tensor, g_subln.offset, [[0, P], [1, HD]])
                           ).then_inc(const_landed, 16)
            with pool.Fori(0, 4) as g:
                pool.wait_ge(ssq_o_ready, g + 1)
                nc.gpsimd.tensor_tensor(ssq_o[:], ssq_o[:], eps[:], ALU.add).then_inc(gsub_pool, 1)
                pool.wait_ge(gsub_pool, g + 1)
                nc.gpsimd.tensor_tensor(rstd_o[:], ssq_o[:], half[:, 0:4].rearrange("p (h t) -> p h t", h=2),
                                        ALU.pow).then_inc(rstd_o_ready, 1)
            for c in range(4):
                pool.wait_ge(slab_used, N_OUT + 3 * c)
                cols = slice(c * (D // 4), (c + 1) * (D // 4))
                pool.dma_start(acc_out[:, :, cols], x[:, cols].rearrange("(t p) n -> p t n", p=P)
                               ).then_inc(resid_landed, 16)
            pool.wait_ge(slab_used, N_OUT + 12)
            pool.dma_start(g_fin[:], bass.AP(g_final.tensor, g_final.offset, [[0, P], [1, D]])
                           ).then_inc(gfin_landed, 16)
            pool.wait_ge(gfin_landed, 16)
            with pool.Fori(0, OUT_JOBS - 1) as n:
                for t in range(T):
                    pool.wait_ge(squared_out, n * 2 + (t + 1))
                    nc.gpsimd.tensor_tensor(acc_out[:, t, ds(n * CH, CH)], acc_out[:, t, ds(n * CH, CH)],
                                            g_fin[:, ds(n * CH, CH)], ALU.mult).then_inc(scaled_out, 1)
            pool.wait_ge(ssq_f_ready, 1)
            nc.gpsimd.tensor_tensor(rstd_f[:], ms_f[:], half[:, 0:T], ALU.pow).then_inc(rstd_f_ready, 1)


_INS = ['x', 'mem', 'g_in', 'w_in', 'g_mem', 'w_mem_k', 'w_mem_v', 'lam_q1', 'lam_k1', 'lam_q2', 'lam_k2',
        'g_subln', 'w_fourier', 'w_out', 'g_final']
_FLAT = {'x', 'mem', 'w_in', 'w_mem_k', 'w_mem_v', 'w_fourier', 'w_out'}


def _constants():
    i = np.arange(SEQ, dtype=np.int64)
    dist = np.abs(i[:, None] - i[None, :]).astype(np.float32)
    slopes = np.array([[-2.0 ** -(h + 1) for h in range(8)]], dtype=np.float32)
    angle = 2.0 * np.pi * ((i[:, None] * i[None, :]) % SEQ).astype(np.float64) / SEQ
    dft = (np.concatenate([np.cos(angle), np.sin(angle)], axis=1) / 16.0).astype(np.float32)
    half = np.concatenate([dft[:, 0:P + 1], dft[:, SEQ + 1:SEQ + P]], axis=1)
    return {'dist': dist, 'slope': slopes, 'dft': dft, 'dft_half': half}


def kernel(**inputs):
    import numpy as _np
    import concourse.bacc as _bacc
    from concourse import mybir as _mybir
    from concourse.bass_utils import run_bass_kernel_spmd as _run

    nc = _bacc.Bacc("TRN2", target_bir_lowering=False, num_devices=1)
    arrays, args = {}, []
    for name in _INS:
        a = _np.ascontiguousarray(inputs[name])
        if name in _FLAT:
            a = a.reshape(a.shape[1:])
        arrays[f"in_{name}_dram"] = a
        args.append(nc.dram_tensor(f"in_{name}_dram", a.shape, _mybir.dt.from_np(a.dtype), kind="ExternalInput").ap())
    for name, a in _constants().items():
        arrays[f"const_{name}_dram"] = a
        args.append(nc.dram_tensor(f"const_{name}_dram", a.shape, _mybir.dt.from_np(a.dtype),
                                   kind="ExternalInput").ap())
    args.append(nc.dram_tensor("out_0_dram", (SEQ, D), _mybir.dt.float32, kind="ExternalOutput").ap())
    hybrid_kernel(nc, *args)
    r = _run(nc, [arrays], core_ids=[0])
    return r.results[0]["out_0_dram"].reshape(1, SEQ, D)
```
